# Optimizing a Trainium2 kernel written in Bass

```python
import jax, jax.numpy as jnp
from jax import lax
import numpy as np

D_MODEL = 1024
BATCH = 1
SEQ = 512
DEPTH = 1

CHUNK = 128
RET_HEADS = 4
RET_DK = 128
RET_DV = 256
RET_QK_W = RET_HEADS * RET_DK
RET_V_W = RET_HEADS * RET_DV
SGU_GROUPS = 4
SGU_W = 1024
SGU_GW = SGU_W // SGU_GROUPS
D_FF = 2816
CONV_W = 3
ROPE_BASE = 10000.0
EPS = 1e-6
IN_SPLITS = (RET_QK_W, RET_QK_W, RET_V_W, RET_V_W, SGU_W, SGU_W, D_MODEL, D_MODEL)
IN_W = sum(IN_SPLITS)


def _rmsnorm(x, g):
    xf = x.astype(jnp.float32)
    y = xf * lax.rsqrt(jnp.mean(xf * xf, axis=-1, keepdims=True) + EPS)
    return (y * g.astype(jnp.float32)).astype(x.dtype)

def _layernorm(x, g=None, b=None):
    xf = x.astype(jnp.float32)
    mu = jnp.mean(xf, axis=-1, keepdims=True)
    var = jnp.mean(jnp.square(xf - mu), axis=-1, keepdims=True)
    y = (xf - mu) * lax.rsqrt(var + EPS)
    if g is not None:
        y = y * g.astype(jnp.float32) + b.astype(jnp.float32)
    return y.astype(x.dtype)

def _rotary(t):
    S, d = t.shape[1], t.shape[-1]
    half = d // 2
    inv_freq = 1.0 / (ROPE_BASE ** (jnp.arange(half, dtype=jnp.float32) / half))
    ang = jnp.arange(S, dtype=jnp.float32)[:, None] * inv_freq[None, :]
    cos = jnp.cos(ang)[None, :, None, :].astype(t.dtype)
    sin = jnp.sin(ang)[None, :, None, :].astype(t.dtype)
    t1, t2 = t[..., :half], t[..., half:]
    return jnp.concatenate([t1 * cos - t2 * sin, t1 * sin + t2 * cos], axis=-1)

def _to_chunks(t):
    B, S, H, d = t.shape
    return t.reshape(B, S // CHUNK, CHUNK, H, d).transpose(0, 3, 1, 2, 4)

def _from_chunks(t):
    B, H, N, C, d = t.shape
    return t.transpose(0, 2, 3, 1, 4).reshape(B, N * C, H, d)

def _retention_one_direction(q, k, v, log_gamma, strict):
    dt = q.dtype
    idx = jnp.arange(CHUNK, dtype=jnp.float32)
    diff = idx[:, None] - idx[None, :]
    mask = (diff > 0) if strict else (diff >= 0)
    lg = log_gamma[:, None, None]
    dmat = jnp.where(mask[None], jnp.exp(jnp.where(mask, diff, 0.0)[None] * lg), 0.0)
    s = jnp.einsum('bhncd,bhnmd->bhncm', q, k) * dmat[None, :, None].astype(dt)
    intra = jnp.einsum('bhncm,bhnme->bhnce', s, v)
    zeta = jnp.exp((CHUNK - 1.0 - idx)[None, :] * log_gamma[:, None]).astype(dt)
    xi = jnp.exp((idx + 1.0)[None, :] * log_gamma[:, None]).astype(dt)
    decay_c = jnp.exp(CHUNK * log_gamma).astype(dt)[None, :, None, None]
    kv = jnp.einsum('bhnmd,bhnme->nbhde', k, v * zeta[None, :, None, :, None])

    def step(state, kv_n):
        return decay_c * state + kv_n, state

    _, r_prev = lax.scan(step, jnp.zeros_like(kv[0]), kv)
    cross = jnp.einsum('bhncd,nbhde->bhnce', q * xi[None, :, None, :, None], r_prev)
    return intra + cross

def _retention_branch(q, k, v, g, ret_decay_logit, w_ret_o):
    B, S, _ = q.shape
    q = _rotary(q.reshape(B, S, RET_HEADS, RET_DK))
    k = _rotary(k.reshape(B, S, RET_HEADS, RET_DK)) * (RET_DK ** -0.5)
    v = v.reshape(B, S, RET_HEADS, RET_DV)
    log_gamma = jax.nn.log_sigmoid(ret_decay_logit.astype(jnp.float32))
    fwd = _retention_one_direction(_to_chunks(q), _to_chunks(k), _to_chunks(v), log_gamma[0], False)
    qb, kb, vb = (jnp.flip(t, axis=1) for t in (q, k, v))
    bwd = _retention_one_direction(_to_chunks(qb), _to_chunks(kb), _to_chunks(vb), log_gamma[1], True)
    o = _from_chunks(fwd) + jnp.flip(_from_chunks(bwd), axis=1)
    o = _layernorm(o).reshape(B, S, RET_V_W)
    return (o * jax.nn.silu(g)) @ w_ret_o

def _sgu_branch(u, sv, sgu_ln_g, sgu_ln_b, w_spatial, b_spatial, w_sgu_o):
    B, S, _ = u.shape
    u = jax.nn.gelu(u)
    sv = _layernorm(jax.nn.gelu(sv), sgu_ln_g, sgu_ln_b)
    svc = sv.reshape(B, S // CHUNK, CHUNK, SGU_GROUPS, SGU_GW)
    mixed = jnp.einsum('gpq,bnqgc->bnpgc', w_spatial, svc) + b_spatial.T[None, None, :, :, None]
    y = u * mixed.reshape(B, S, SGU_W)
    return y @ w_sgu_o

def _conv_gated_mlp(h, w_up, conv_w, conv_b, w_down):
    hid = h @ w_up
    c = hid.shape[-1]
    hid = lax.conv_general_dilated(
        hid, conv_w.reshape(CONV_W, 1, c), window_strides=(1,),
        padding=((CONV_W // 2, CONV_W // 2),),
        dimension_numbers=('NWC', 'WIO', 'NWC'), feature_group_count=c) + conv_b
    a, b = jnp.split(hid, 2, axis=-1)
    return (jax.nn.gelu(a) * b) @ w_down

def first_inputs(seed: int = 0) -> dict:
    key = jax.random.key(seed)
    ks = jax.random.split(key, 20)
    f32 = jnp.float32
    nrm = lambda k, shape, s: jax.random.normal(k, shape, f32) * s
    gamma0 = 1.0 - 2.0 ** (-5.0 - np.arange(RET_HEADS, dtype=np.float32))
    logit0 = jnp.asarray(np.log(gamma0) - np.log1p(-gamma0), f32)
    return {
        "x": nrm(ks[0], (BATCH, SEQ, D_MODEL), 1.0),
        "g_pre_mix": 1.0 + nrm(ks[1], (D_MODEL,), 0.05),
        "w_in": nrm(ks[2], (D_MODEL, IN_W), D_MODEL ** -0.5),
        "ret_decay_logit": logit0[None, :] + nrm(ks[3], (2, RET_HEADS), 0.1),
        "sgu_ln_g": 1.0 + nrm(ks[4], (SGU_W,), 0.05),
        "sgu_ln_b": nrm(ks[5], (SGU_W,), 0.02),
        "w_spatial": nrm(ks[6], (SGU_GROUPS, CHUNK, CHUNK), CHUNK ** -0.5),
        "b_spatial": nrm(ks[7], (SGU_GROUPS, CHUNK), 0.02),
        "w_ret_o": nrm(ks[8], (RET_V_W, D_MODEL), RET_V_W ** -0.5),
        "w_sgu_o": nrm(ks[9], (SGU_W, D_MODEL), SGU_W ** -0.5),
        "w_out": nrm(ks[10], (D_MODEL, D_MODEL), D_MODEL ** -0.5),
        "g_post_mix": 1.0 + nrm(ks[11], (D_MODEL,), 0.05),
        "g_pre_ffn": 1.0 + nrm(ks[12], (D_MODEL,), 0.05),
        "w_up": nrm(ks[13], (D_MODEL, 2 * D_FF), D_MODEL ** -0.5),
        "conv_w": nrm(ks[14], (CONV_W, 2 * D_FF), CONV_W ** -0.5),
        "conv_b": nrm(ks[15], (2 * D_FF,), 0.02),
        "w_down": nrm(ks[16], (D_FF, D_MODEL), D_FF ** -0.5),
        "g_post_ffn": 1.0 + nrm(ks[17], (D_MODEL,), 0.05),
    }

def first_block(x, g_pre_mix, w_in, ret_decay_logit, sgu_ln_g, sgu_ln_b, w_spatial, b_spatial,
              w_ret_o, w_sgu_o, w_out, g_post_mix, g_pre_ffn, w_up, conv_w, conv_b, w_down,
              g_post_ffn):
    for _ in range(DEPTH):
        h = _rmsnorm(x, g_pre_mix)
        proj = h @ w_in
        q, k, v, g, u, sv, a_ret, a_sgu = jnp.split(proj, list(np.cumsum(IN_SPLITS)[:-1]), axis=-1)
        y_ret = _retention_branch(q, k, v, g, ret_decay_logit, w_ret_o)
        y_sgu = _sgu_branch(u, sv, sgu_ln_g, sgu_ln_b, w_spatial, b_spatial, w_sgu_o)
        merged = jax.nn.sigmoid(a_ret) * y_ret + jax.nn.sigmoid(a_sgu) * y_sgu
        x = x + _rmsnorm(merged @ w_out, g_post_mix)
        h2 = _rmsnorm(x, g_pre_ffn)
        x = x + _rmsnorm(_conv_gated_mlp(h2, w_up, conv_w, conv_b, w_down), g_post_ffn)
    return x


HEAD_DIM = 64
A_HEADS = 8
A_KV_HEADS = 2
IDX_HEADS = 8
IDX_DIM = 64
TOPK_MAX = 256
B_HEADS = 8
B_KV_HEADS = 2
WINDOW = 128
Q_BLOCK = 128
D_FF_2 = 4 * D_MODEL
ROPE_THETA = 10000.0
RMS_EPS = 1e-6
LN_EPS = 1e-6

A_Q = A_HEADS * HEAD_DIM
A_KV = A_KV_HEADS * HEAD_DIM
IDX_Q = IDX_HEADS * IDX_DIM
B_Q = B_HEADS * HEAD_DIM
B_KV = B_KV_HEADS * HEAD_DIM
SPLIT_SIZES = (A_Q, A_KV, A_KV, IDX_Q, IDX_DIM, IDX_HEADS, B_Q, B_KV, B_KV, D_MODEL, D_MODEL)
D_IN = sum(SPLIT_SIZES)


def rmsnorm(x, g):
    xf = x.astype(jnp.float32)
    y = xf * lax.rsqrt(jnp.mean(xf * xf, axis=-1, keepdims=True) + RMS_EPS)
    return (y * g.astype(jnp.float32)).astype(x.dtype)

def layernorm(x, w, b):
    xf = x.astype(jnp.float32)
    mu = jnp.mean(xf, axis=-1, keepdims=True)
    var = jnp.mean(jnp.square(xf - mu), axis=-1, keepdims=True)
    y = (xf - mu) * lax.rsqrt(var + LN_EPS)
    return (y * w.astype(jnp.float32) + b.astype(jnp.float32)).astype(x.dtype)

def rope_tables(L, dim):
    inv = 1.0 / (ROPE_THETA ** (jnp.arange(0, dim, 2, dtype=jnp.float32) / dim))
    ang = jnp.arange(L, dtype=jnp.float32)[:, None] * inv[None, :]
    return jnp.cos(ang), jnp.sin(ang)

def apply_rope(x, cos, sin):
    xf = x.astype(jnp.float32)
    x1, x2 = jnp.split(xf, 2, axis=-1)
    c = cos[None, :, None, :]
    s = sin[None, :, None, :]
    return jnp.concatenate([x1 * c - x2 * s, x2 * c + x1 * s], axis=-1).astype(x.dtype)

def dsa_branch(q, k, v, q_idx, k_idx, w_idx, topk):
    Bn, L, H, dh = q.shape
    G = k.shape[2]
    R = H // G
    nb = L // Q_BLOCK
    kpos = jnp.arange(L)
    k_idx32 = k_idx.astype(jnp.float32)
    scale = HEAD_DIM ** -0.5

    def one_block(i):
        start = i * Q_BLOCK
        qb = lax.dynamic_slice_in_dim(q, start, Q_BLOCK, axis=1)
        qib = lax.dynamic_slice_in_dim(q_idx, start, Q_BLOCK, axis=1)
        wb = lax.dynamic_slice_in_dim(w_idx, start, Q_BLOCK, axis=1)
        qpos = start + jnp.arange(Q_BLOCK)
        s = jnp.einsum('bqhd,bkd->bqhk', qib.astype(jnp.float32), k_idx32)
        score = jnp.einsum('bqhk,bqh->bqk', jax.nn.relu(s), wb.astype(jnp.float32))
        causal = kpos[None, :] <= qpos[:, None]
        score = jnp.where(causal[None], score, -jnp.inf)
        _, sel = lax.top_k(score, topk)
        ks = jax.vmap(lambda kk, ii: kk[ii])(k, sel)
        vs = jax.vmap(lambda vv, ii: vv[ii])(v, sel)
        valid = sel <= qpos[None, :, None]
        qg = qb.reshape(Bn, Q_BLOCK, G, R, dh).astype(jnp.float32)
        logits = jnp.einsum('bqgrd,bqkgd->bqgrk', qg, ks.astype(jnp.float32)) * scale
        logits = jnp.where(valid[:, :, None, None, :], logits, -jnp.inf)
        p = jax.nn.softmax(logits, axis=-1)
        o = jnp.einsum('bqgrk,bqkgd->bqgrd', p, vs.astype(jnp.float32))
        return o.reshape(Bn, Q_BLOCK, H * dh).astype(q.dtype)

    out = lax.map(one_block, jnp.arange(nb))
    return jnp.transpose(out, (1, 0, 2, 3)).reshape(Bn, L, H * dh)

def swa_branch(q, k, v, sinks):
    Bn, L, H, dh = q.shape
    G = k.shape[2]
    R = H // G
    W = WINDOW
    nb = L // W
    qb = q.reshape(Bn, nb, W, G, R, dh).astype(jnp.float32)
    pad = ((0, 0), (W, 0), (0, 0), (0, 0))
    kp = jnp.pad(k, pad).reshape(Bn, nb + 1, W, G, dh)
    vp = jnp.pad(v, pad).reshape(Bn, nb + 1, W, G, dh)
    kb = jnp.concatenate([kp[:, :-1], kp[:, 1:]], axis=2).astype(jnp.float32)
    vb = jnp.concatenate([vp[:, :-1], vp[:, 1:]], axis=2).astype(jnp.float32)
    logits = jnp.einsum('bnqgrd,bnkgd->bngrqk', qb, kb) * (HEAD_DIM ** -0.5)
    rel = jnp.arange(W)[:, None] + W - jnp.arange(2 * W)[None, :]
    kabs = jnp.arange(nb)[:, None] * W - W + jnp.arange(2 * W)[None, :]
    mask = ((rel >= 0) & (rel < W))[None, :, :] & (kabs >= 0)[:, None, :]
    logits = jnp.where(mask[None, :, None, None, :, :], logits, -jnp.inf)
    sink = jnp.broadcast_to(sinks.astype(jnp.float32).reshape(1, 1, G, R, 1, 1), logits.shape[:-1] + (1,))
    p = jax.nn.softmax(jnp.concatenate([logits, sink], axis=-1), axis=-1)[..., :-1]
    o = jnp.einsum('bngrqk,bnkgd->bnqgrd', p, vb)
    return o.reshape(Bn, L, H * dh).astype(q.dtype)

def second_inputs(seed: int = 0) -> dict:
    key = jax.random.key(seed)
    ks = jax.random.split(key, 14)
    f32 = jnp.float32
    nrm = lambda k, shape: jax.random.normal(k, shape, dtype=f32)
    return {
        "x": nrm(ks[0], (BATCH, SEQ, D_MODEL)),
        "attn_norm_w": 1.0 + 0.02 * nrm(ks[1], (DEPTH, D_MODEL)),
        "w_in": nrm(ks[2], (DEPTH, D_MODEL, D_IN)) * D_MODEL ** -0.5,
        "idx_k_norm_w": 1.0 + 0.02 * nrm(ks[3], (DEPTH, IDX_DIM)),
        "idx_k_norm_b": 0.02 * nrm(ks[4], (DEPTH, IDX_DIM)),
        "sinks": 0.5 * nrm(ks[5], (DEPTH, B_HEADS)),
        "w_branch_a": nrm(ks[6], (DEPTH, A_Q, D_MODEL)) * A_Q ** -0.5,
        "w_branch_b": nrm(ks[7], (DEPTH, B_Q, D_MODEL)) * B_Q ** -0.5,
        "w_out": nrm(ks[8], (DEPTH, D_MODEL, D_MODEL)) * D_MODEL ** -0.5,
        "mlp_norm_w": 1.0 + 0.02 * nrm(ks[9], (DEPTH, D_MODEL)),
        "w_up": nrm(ks[10], (DEPTH, D_MODEL, D_FF_2)) * D_MODEL ** -0.5,
        "w_down": nrm(ks[11], (DEPTH, D_FF_2, D_MODEL)) * D_FF_2 ** -0.5,
        "final_norm_w": 1.0 + 0.02 * nrm(ks[12], (D_MODEL,)),
    }

def second_block(x, attn_norm_w, w_in, idx_k_norm_w, idx_k_norm_b, sinks, w_branch_a, w_branch_b,
              w_out, mlp_norm_w, w_up, w_down, final_norm_w):
    Bn, L, _ = x.shape
    topk = min(TOPK_MAX, L // 4)
    cos, sin = rope_tables(L, HEAD_DIM)
    cos_i, sin_i = rope_tables(L, IDX_DIM)
    offsets = [sum(SPLIT_SIZES[:i + 1]) for i in range(len(SPLIT_SIZES) - 1)]
    w_scale = (IDX_HEADS ** -0.5) * (IDX_DIM ** -0.5)

    for l in range(DEPTH):
        h = rmsnorm(x, attn_norm_w[l])
        proj = jnp.einsum('bld,de->ble', h, w_in[l])
        a_q, a_k, a_v, i_q, i_k, i_w, b_q, b_k, b_v, g_a, g_b = jnp.split(proj, offsets, axis=-1)

        a_q = apply_rope(a_q.reshape(Bn, L, A_HEADS, HEAD_DIM), cos, sin)
        a_k = apply_rope(a_k.reshape(Bn, L, A_KV_HEADS, HEAD_DIM), cos, sin)
        a_v = a_v.reshape(Bn, L, A_KV_HEADS, HEAD_DIM)
        i_q = apply_rope(i_q.reshape(Bn, L, IDX_HEADS, IDX_DIM), cos_i, sin_i)
        i_k = layernorm(i_k, idx_k_norm_w[l], idx_k_norm_b[l])
        i_k = apply_rope(i_k[:, :, None, :], cos_i, sin_i)[:, :, 0, :]
        i_w = i_w * w_scale
        o_a = dsa_branch(a_q, a_k, a_v, i_q, i_k, i_w, topk)

        b_q = apply_rope(b_q.reshape(Bn, L, B_HEADS, HEAD_DIM), cos, sin)
        b_k = apply_rope(b_k.reshape(Bn, L, B_KV_HEADS, HEAD_DIM), cos, sin)
        b_v = b_v.reshape(Bn, L, B_KV_HEADS, HEAD_DIM)
        o_b = swa_branch(b_q, b_k, b_v, sinks[l])

        y_a = jnp.einsum('ble,ed->bld', o_a, w_branch_a[l])
        y_b = jnp.einsum('ble,ed->bld', o_b, w_branch_b[l])
        mix = jax.nn.sigmoid(g_a) * y_a + jax.nn.sigmoid(g_b) * y_b
        x = x + jnp.einsum('bld,de->ble', mix, w_out[l])

        h2 = rmsnorm(x, mlp_norm_w[l])
        u = jax.nn.relu(jnp.einsum('bld,df->blf', h2, w_up[l]))
        x = x + jnp.einsum('blf,fd->bld', u * u, w_down[l])

    return rmsnorm(x, final_norm_w)


def setup_inputs(seed=0):
    out = dict(first_inputs(seed))
    for name, value in second_inputs(seed + 1).items():
        if name != "x":
            out[name + "_2"] = value
    return out


def reference(
    x, g_pre_mix, w_in, ret_decay_logit, sgu_ln_g, sgu_ln_b, w_spatial, b_spatial, w_ret_o,
    w_sgu_o, w_out, g_post_mix, g_pre_ffn, w_up, conv_w, conv_b, w_down, g_post_ffn,
    attn_norm_w_2, w_in_2, idx_k_norm_w_2, idx_k_norm_b_2, sinks_2, w_branch_a_2, w_branch_b_2,
    w_out_2, mlp_norm_w_2, w_up_2, w_down_2, final_norm_w_2,
):
    x = first_block(
        x, g_pre_mix, w_in, ret_decay_logit, sgu_ln_g, sgu_ln_b, w_spatial, b_spatial, w_ret_o,
        w_sgu_o, w_out, g_post_mix, g_pre_ffn, w_up, conv_w, conv_b, w_down, g_post_ffn,
    )
    return second_block(
        x, attn_norm_w_2, w_in_2, idx_k_norm_w_2, idx_k_norm_b_2, sinks_2, w_branch_a_2,
        w_branch_b_2, w_out_2, mlp_norm_w_2, w_up_2, w_down_2, final_norm_w_2,
    )


_drawn_inputs = setup_inputs


def setup_inputs(seed=0):
    import zlib

    import numpy as np

    out = dict(_drawn_inputs(seed))
    spreads = {}
    factors = {'sgu_ln_b': 3.733,
     'b_spatial': 4.121,
     'conv_b': 3.042,
     'attn_norm_w_2': 8.0,
     'idx_k_norm_w_2': 8.0,
     'idx_k_norm_b_2': 8.0,
     'sinks_2': 41.012,
     'mlp_norm_w_2': 4.093,
     'final_norm_w_2': 8.05}
    for name, (base, spread) in spreads.items():
        noise = np.random.default_rng([zlib.crc32(name.encode()), seed]).standard_normal(out[name].shape)
        drawn = base * np.exp(spread * noise) if base else spread * noise
        out[name] = __import__('jax').numpy.asarray(drawn.astype(out[name].dtype))
    for name, factor in factors.items():
        out[name] = (out[name] * factor).astype(out[name].dtype)
    return out
```

```python
import math

import concourse.bass as bass
from concourse import mybir
from contextlib import ExitStack

P = 128
D = 1024
S = 512
NT = S // P
KT = D // P
RET_H, RET_DK, RET_DV = 4, 128, 256
SGU_G = 4
FF = 2816
FB = FF // P
FF2 = 4096
HD = 64
HEADS, KV_HEADS = 8, 2
TOPK = min(256, S // 4)
EPS = 1e-6
NEG = -1.0e30
LOWEST = -3.0e38
STRIP = (2 * NT - 1) * P

IN1_G = 2 * RET_H * RET_DK + RET_H * RET_DV
IN1_U = IN1_G + RET_H * RET_DV
IN1_SV = IN1_U + D
IN1_AR = IN1_SV + D
IN1_AS = IN1_AR + D
IN2_AK = 512
IN2_IQ2 = 1024
IN2_BQ = 1352
IN2_BK = 1864
IN2_GA = 2120
IN2_GB = 3144
IB_W = IN2_BQ - IN2_IQ2


def attention_events():
    events = []
    pairs = NT * HEADS
    for s in range(pairs + 7):
        if s < pairs:
            events.append(("logits", s))
        if 0 <= s - 3 < pairs:
            events.append(("probs_T", s - 3))
        if 0 <= s - 4 < pairs:
            events.append(("values", s - 4))
        done = s - 6
        if done > 0 and done % HEADS == HEADS - 1 and done < pairs:
            events.append(("out_T", done // HEADS))
    return events


ATTENTION = attention_events()
RETENTION = [("scores", 0), ("scores", 1), ("values", 0), ("scores", 2), ("values", 1),
             ("scores", 3), ("values", 2), ("values", 3)]

TICKETS = [("h1", 8), ("conv_cols", 1), ("spatial_T", 1), ("qkvg", 24), ("qk_T", 8), ("ret", 24), ("sv", 8),
           ("u", 8), ("o_T", 8), ("mix", 8), ("a_ret", 8), ("y_ret", 8), ("a_sgu", 8), ("y_sgu", 8),
           ("out1", 8), ("h2", 8), ("up1", 2 * FB), ("down1", 8), ("h3", 8),
           ("kv_iq", 4), ("iq_ik", 4), ("b_q", 4), ("i_T", 5), ("b_kv", 4), ("index", 24),
           ("g_b", 8), ("g_a", 8), ("b_T", 5), ("a_q", 4), ("swa", 100), ("y_b", 8), ("a_T", 5),
           ("dsa", 100), ("y_a", 8), ("out2", 8), ("h4", 8),
           ("up2_0", 16), ("down2_0", 8), ("up2_1", 16), ("down2_1", 8)]
UNITS = [("qkvg", 12), ("sv", 4), ("u", 4), ("a_ret", 4), ("y_ret", 4), ("a_sgu", 4), ("y_sgu", 4),
         ("out1", 4), ("up1", FB), ("down1", FB // 2), ("kv_iq", 2), ("iq_ik", 2), ("b_q", 2),
         ("b_kv", 1), ("g_b", 4), ("g_a", 4), ("a_q", 2), ("y_b", 2), ("y_a", 2), ("out2", 4),
         ("up2_0", 8), ("down2_0", 8), ("up2_1", 8), ("down2_1", 8)]


def starts(parts):
    at, out = 0, {}
    for name, n in parts:
        out[name] = at
        at += n
    return out, at


T0, _ = starts(TICKETS)
U0, N_UNITS = starts(UNITS)
UNIT = 2048


class Count:

    def __init__(self, engine, sem):
        self.engine, self.sem, self.n = engine, sem, 0

    def up(self, instruction):
        instruction.then_inc(self.sem, 1)
        self.n += 1

    def wait(self):
        if self.n:
            self.engine.wait_ge(self.sem, self.n)

    def take(self, n=1):
        self.n += n
        self.engine.wait_ge(self.sem, self.n)


def two_blocks(nc: bass.Bass, a, out: bass.AP):
    f32 = mybir.dt.float32
    f32r = mybir.dt.float32r
    ALU = mybir.AluOpType
    ACT = mybir.ActivationFunctionType

    ctx = ExitStack()
    with ctx:
        BASE = (nc.sbuf_base + 31) // 32 * 32
        KB = 1024

        def at(name, shape, offset, dt=f32):
            return nc.alloc_sbuf_tensor_at(name, shape, dt, offset=int(BASE + offset))

        x = at("x", [P, NT, D], 0)
        hT_hi = at("hT_hi", [P, KT, S], 16 * KB, f32r)
        hT_lo = at("hT_lo", [P, KT, S], 32 * KB, f32r)
        raw = at("raw", [P, 2, UNIT], 48 * KB)
        w_hi = at("w_hi", [P, 2, UNIT], 64 * KB, f32r)
        w_lo = at("w_lo", [P, 2, UNIT], 80 * KB, f32r)
        gain = at("gain", [P, 2, D], 96 * KB)
        mask = at("mask", [P, NT, S], 96 * KB)
        small0 = 104 * KB
        ident = at("ident", [P, P], small0)
        rope2 = at("rope2", [P, NT, 3, HD // 2], small0 + 512)
        band = at("band", [P, 2 * P], small0 + 2048)
        conv = at("conv", [P, 4, 2 * FB], small0 + 3072)
        cells = at("cells", [P, 192], small0 + 3776)
        A = small0 + 3776 + 768
        eps = cells[:, 0:1]
        rms = cells[:, 160:168]
        rstd = cells[:, 168:176]
        sq = cells[:, 4:8]
        sink = cells[:, 8:16]
        nsink = cells[:, 16:24]
        lg = cells[:, 24:32]
        nm = cells[:, 32:48].rearrange("p (t h) -> p t h", t=2)
        rs = cells[:, 48:64].rearrange("p (t h) -> p t h", t=2)
        ri = cells[:, 64:80].rearrange("p (t h) -> p t h", t=2)
        sink_e = cells[:, 80:96].rearrange("p (t h) -> p t h", t=2)
        zero = cells[:, 176:177]
        gm = [cells[:, 96 + 8 * n:104 + 8 * n] for n in range(8)]

        v = at("v", [P, NT, RET_H * RET_DV], A)
        silu_g = at("silu_g", [P, NT, D], A + 16 * KB)
        qk = at("qk", [P, 2, NT, S], A + 32 * KB)
        o = at("o", [P, NT, RET_H, RET_DV], A + 32 * KB)
        qT = at("qT", [P, RET_H, S], A + 48 * KB)
        kT = at("kT", [P, RET_H, S], A + 56 * KB)
        sT = at("sT", [P, 2, NT, S], A + 64 * KB)
        rope_t = at("rope_t", [P, 2, S], A + 64 * KB)
        decay = at("decay", [P, 3, STRIP], A + 80 * KB)
        o_stat = at("o_stat", [P, 104], A + int(92.5 * KB))
        sv_stat = at("sv_stat", [P, 72], A + 87 * KB)
        spatial_T = at("spatial_T", [P, SGU_G, P], A + int(90.5 * KB))
        spatial = at("spatial", [P, SGU_G, P], A)
        conv_rows = at("conv_rows", [2 * FB, 4, P], A + 2 * KB)
        sv = at("sv", [P, NT, D], A + 48 * KB)
        uT = at("uT", [P, KT, S], A + 64 * KB)
        spatial_b = at("spatial_b", [P, SGU_G, P], A + 80 * KB)
        mix_t = at("mix_t", [P, 2, S], A + 82 * KB)
        oT_hi = at("oT_hi", [P, KT, S], A, f32r)
        oT_lo = at("oT_lo", [P, KT, S], A + 16 * KB, f32r)
        yT_hi = at("yT_hi", [P, KT, S], A + 32 * KB, f32r)
        yT_lo = at("yT_lo", [P, KT, S], A + 64 * KB, f32r)
        mT = at("mT", [P, KT, S], A + 48 * KB)
        mT_lo = at("mT_lo", [P, KT, S], A + 48 * KB, f32r)
        mT_hi = at("mT_hi", [P, KT, S], A + 16 * KB, f32r)
        sgu_gate = at("sgu_gate", [P, KT, S], A)
        tables0 = A + 101792 - 6656
        distance = at("distance", [P, STRIP], tables0)
        rope1 = at("rope1", [P, NT, 3, RET_DK // 2], tables0 + 4 * STRIP)
        slot1 = at("slot1", [P, 2, D], A + 64 * KB)
        f_hi = at("f_hi", [P, FB, S], A, f32r)
        f_lo = at("f_lo", [P, FB, S], A + 44 * KB, f32r)
        taps = at("taps", [P, 2, 2, S], A + 88 * KB)
        slot2 = at("slot2", [P, 2, D], A + 88 * KB)
        kn = at("kn", [P, NT, S], A)
        ib = at("ib", [P, NT, IB_W], A + 8 * KB)
        qn = at("qn", [P, NT, S], A + int(13.5 * KB))
        bkv = at("bkv", [P, NT, 2 * P], A + int(21.5 * KB))
        qT_a = at("qT_a", [P, NT, S], A + int(25.5 * KB))
        ikT = at("ikT", [P, S], A + int(33.5 * KB))
        akT = at("akT", [P, S], A + int(35.5 * KB))
        qT_b = at("qT_b", [P, NT, S], A + int(37.5 * KB))
        bkT = at("bkT", [P, S], A + int(45.5 * KB))
        score = at("score", [P, S], A + int(47.5 * KB))
        work = at("work", [P, S], A + int(49.5 * KB))
        relu = at("relu", [P, 2, S], A + int(51.5 * KB))
        rope_u = at("rope_u", [P, 2, S], A + int(51.5 * KB))
        probs = at("probs", [P, 4, S], A + int(47.5 * KB))
        probs_T = at("probs_T", [P, 2, S], A + int(55.5 * KB))
        o2 = at("o2", [P, 2, S], A + int(59.5 * KB))
        above = at("above", [P, S], A + int(55.5 * KB))
        equal = at("equal", [P, S], A + int(57.5 * KB))
        upto = at("upto", [P, S], A + int(59.5 * KB))
        ik2 = at("ik2", [P, NT, 2, HD], A + int(61.5 * KB))
        ik_gain = at("ik_gain", [P, 2, HD], A + int(63.5 * KB))
        ik_stat = at("ik_stat", [P, 64], A + 64 * KB)
        top = at("top", [P, 16], A + int(64.5 * KB))
        sig_b = at("sig_b", [P, KT, S], A + int(65.5 * KB))
        sig_a = at("sig_a", [P, KT, S], A + int(81.5 * KB))
        m2_lo = at("m2_lo", [P, KT, S], A + int(81.5 * KB), f32r)
        m2_hi = at("m2_hi", [P, KT, S], A, f32r)
        oTb_hi = at("oTb_hi", [P, NT, S], 16 * KB, f32r)
        oTb_lo = at("oTb_lo", [P, NT, S], 24 * KB, f32r)
        oTa_hi = at("oTa_hi", [P, NT, S], 32 * KB, f32r)
        oTa_lo = at("oTa_lo", [P, NT, S], 40 * KB, f32r)
        slot3 = at("slot3", [P, 2, D], A + 48 * KB)
        f2_hi = at("f2_hi", [P, 16, S], A, f32r)
        f2_lo = at("f2_lo", [P, 16, S], A + 32 * KB, f32r)
        f2_t = at("f2_t", [P, 4, S], A + 64 * KB)
        slot4 = at("slot4", [P, 2, D], A + 72 * KB)

        ps = ctx.enter_context(nc.psum_tensor("ps", [P, 8, S], f32))

        def sem(name):
            return ctx.enter_context(nc.semaphore(name))

        x_loaded = [sem(f"x_loaded{t}") for t in range(NT)]
        tables_loaded = sem("tables_loaded")
        gains_loaded = sem("gains_loaded")
        raw_loaded = [sem(f"raw_loaded{s}") for s in range(2)]
        unit_hi = sem("unit_hi")
        unit_split = sem("unit_split")
        unit_started = sem("unit_started")
        psum_ready = sem("psum_ready")
        evacuated = [sem(f"evacuated{b}") for b in range(8)]
        dve_step = sem("dve_step")
        act_step = sem("act_step")
        eps_set = sem("eps_set")
        zero_set = sem("zero_set")
        rms_made = sem("rms_made")
        x_updated = sem("x_updated")
        h_made = sem("h_made")
        hi_made = sem("hi_made")
        spatial_b_loaded = sem("spatial_b_loaded")
        ik_gain_loaded = sem("ik_gain_loaded")
        ident_loaded = sem("ident_loaded")
        hot = sem("hot")
        lo_made = sem("lo_made")
        gamma_arg = sem("gamma_arg")
        gamma_exp = sem("gamma_exp")
        decay_arg = sem("decay_arg")
        decay_made = sem("decay_made")
        qk_rotated = sem("qk_rotated")
        o_stats = sem("o_stats")
        o_rms = sem("o_rms")
        o_gated = sem("o_gated")
        sv_stats = sem("sv_stats")
        sv_rms = sem("sv_rms")
        sv_normed = sem("sv_normed")
        centre = sem("centre")
        left = sem("left")
        gelu_made = sem("gelu_made")
        gated = sem("gated")
        f_hi_made = sem("f_hi_made")
        f_made = sem("f_made")
        ik_stats = sem("ik_stats")
        ik_rms = sem("ik_rms")
        i_rotated = sem("i_rotated")
        b_rotated = sem("b_rotated")
        a_rotated = sem("a_rotated")
        probs_made = sem("probs_made")
        sinks_arg = sem("sinks_arg")
        sinks_exp = sem("sinks_exp")
        o2_made = sem("o2_made")
        squared = sem("squared")
        f2_hi_made = sem("f2_hi_made")
        f2_made = sem("f2_made")
        out_made = sem("out_made")
        stored = [sem(f"stored{s}") for s in range(2)]

        def bank(t):
            return ps[:, t % 8, :]

        def await_psum(engine, t, i=0):
            engine.wait_ge(psum_ready, i * 8 + (t + 1))

        def await_evacuated(engine, t, i=0):
            engine.wait_ge(evacuated[t % 8], i + (t // 8 + 1))

        block = ctx.enter_context(nc.Block())

        @block.sync
        def _(sp):
            def load(u, src, k, i=0, per=0):
                if u >= 2 or per:
                    sp.wait_ge(unit_split, i * (2 * per) + 2 * (u - 1))
                if len(src.shape) == 4:
                    dst = raw[:, u % 2, :].rearrange("p (k h n) -> p k h n", k=k, h=2)
                    parts = [(dst[:, :, h, :], src[:, :, h, :]) for h in range(2)]
                else:
                    dst = raw[:, u % 2, 0:k * src.shape[2]].rearrange("p (k n) -> p k n", k=k)
                    parts = [(dst[:, h:h + k // 2, :], src[:, h:h + k // 2, :]) for h in (0, k // 2)]
                for part, of in parts:
                    sp.dma_start(part, of).then_inc(raw_loaded[u % 2], 16)

            for t in range(NT):
                sp.dma_start(x[:, t, :], a["x"][0, t * P:(t + 1) * P, :]).then_inc(x_loaded[t], 16)
                if t == 0:
                    sp.dma_start(gain[:, 0, :], a["g_pre_mix"].partition_broadcast(P)).then_inc(gains_loaded, 16)
                    sp.dma_start(ident[:, :], a["ident"]).then_inc(ident_loaded, 16)

            def rows(name):
                return a[name].rearrange("(k p) n -> p k n", p=P)

            def wide(name, c, n=512):
                w = rows(name)
                return [w[:, h * 4:h * 4 + 4, c:c + n] for h in range(2)]

            w1 = rows("w_in")
            u = U0["qkvg"]
            for h, src in enumerate(wide("w_in", 0)):
                load(u + h, src, 4)
            for src, dst in ((a["rope1"], rope1), (a["distance"], distance), (a["rope2"], rope2), (a["band"], band)):
                sp.dma_start(dst[:], src).then_inc(tables_loaded, 16)
            sp.dma_start(lg, a["ret_decay_logit"].rearrange("a h -> (a h)").partition_broadcast(P)).then_inc(tables_loaded, 16)
            sp.dma_start(sink, a["sinks"][0, :].partition_broadcast(P)).then_inc(tables_loaded, 16)
            sp.dma_start(spatial[:, :, :], a["w_spatial"].rearrange("g p q -> p g q")).then_inc(tables_loaded, 16)
            sp.dma_start(conv_rows[:, 0:3, :], a["conv_w"].rearrange("t (j c) -> j t c", c=P)).then_inc(tables_loaded, 16)
            sp.dma_start(conv_rows[:, 3, :], a["conv_b"].rearrange("(j c) -> j c", c=P)).then_inc(tables_loaded, 16)
            for h, src in enumerate(wide("w_in", 512)):
                load(u + 2 + h, src, 4)
            with sp.Fori(1, 3) as i:
                for b in range(2):
                    for h in range(2):
                        load(u + 2 * b + h, w1[:, h * 4:h * 4 + 4, bass.ds(i * 1024 + b * 512, 512)], 4, i, 4)
            for b in range(2):
                for h, src in enumerate(wide("w_in", IN1_SV + b * 512)):
                    load(U0["sv"] + 2 * b + h, src, 4)

            def narrow(phase, name, c):
                for j in range(4):
                    load(U0[phase] + j, rows(name)[:, :, c + j * 256:c + j * 256 + 256], KT)

            narrow("u", "w_in", IN1_U)
            narrow("a_ret", "w_in", IN1_AR)
            narrow("y_ret", "w_ret_o", 0)
            narrow("a_sgu", "w_in", IN1_AS)
            narrow("y_sgu", "w_sgu_o", 0)

            def long(phase, name, n, row0=0):
                w = rows(name)
                with sp.Fori(0, n // 2) as i:
                    for j in range(2):
                        load(U0[phase] + j, w[:, bass.ds(i * 4 + (row0 + 2 * j), 2), :], 2, i, 2)
                if n % 2:
                    load(U0[phase] + n - 1, w[:, row0 + 2 * n - 2:row0 + 2 * n, :], 2)

            long("out1", "w_out", 4)
            up = a["w_up"].rearrange("(k p) (h j n) -> p k h j n", p=P, h=2, n=P)
            with sp.Fori(0, FB // 2) as i:
                for j in range(2):
                    load(U0["up1"] + j, up[:, :, :, bass.ds(i * 2 + j, 1), :].rearrange("p k h a n -> p k h (a n)"), KT, i, 2)
            long("down1", "w_down", FB // 2)

            for phase, c, n in (("kv_iq", IN2_AK, 512), ("iq_ik", IN2_IQ2, IB_W), ("b_q", IN2_BQ, 512)):
                for h, src in enumerate(wide("w_in2", c, n)):
                    load(U0[phase] + h, src, 4)
            load(U0["b_kv"], rows("w_in2")[:, :, IN2_BK:IN2_GA], KT)
            narrow("g_b", "w_in2", IN2_GB)
            narrow("g_a", "w_in2", IN2_GA)
            for h, src in enumerate(wide("w_in2", 0)):
                load(U0["a_q"] + h, src, 4)
            for phase, name in (("y_b", "w_branch_b"), ("y_a", "w_branch_a")):
                for j in range(2):
                    load(U0[phase] + j, rows(name)[:, :, j * 512:j * 512 + 512], 4)
            long("out2", "w_out2", 4)
            w_up2 = rows("w_up2")
            for half in range(2):
                with sp.Fori(0, 4) as i:
                    for j in range(2):
                        load(U0[f"up2_{half}"] + j,
                             w_up2[:, :, bass.ds(i * 512 + (half * 2048 + j * 256), 256)], KT, i, 2)
                long(f"down2_{half}", "w_down2", 8, 16 * half)
            for t in range(NT):
                sp.wait_ge(out_made, t + 1)
                sp.dma_start(out[0, t * P:(t + 1) * P, :], slot4[:, t % 2, :]).then_inc(stored[t % 2], 16)
            for s in range(2):
                sp.wait_ge(stored[s], 32)

        @block.gpsimd
        def _(pool):
            def split(u, i=0):
                s = u % 2
                pool.wait_ge(raw_loaded[s], i * 32 + 32)
                if u >= 2:
                    pool.wait_ge(unit_started, i * 2 + s)
                nc.gpsimd.tensor_tensor(w_hi[:, s, :], raw[:, s, :], zero.broadcast_to([P, UNIT]),
                                        ALU.add).then_inc(unit_hi, 1)
                for half in range(2):
                    c = slice(half * UNIT // 2, (half + 1) * UNIT // 2)
                    if half == 0:
                        pool.wait_ge(unit_hi, i * 2 + (s + 1))
                    nc.gpsimd.tensor_tensor(w_lo[:, s, c], raw[:, s, c], w_hi[:, s, c].bitcast(f32),
                                            ALU.subtract).then_inc(unit_split, 1)

            nc.gpsimd.memset(zero, 0.0).then_inc(zero_set, 1)
            pool.wait_ge(zero_set, 1)
            split(0)
            split(1)
            with pool.Fori(1, N_UNITS // 2) as i:
                for s in range(2):
                    split(2 + s, i)

        @block.tensor
        def _(pe):
            h_in = Count(pe, h_made)

            def claim(t, i=0):
                if t >= 8:
                    pe.wait_ge(evacuated[t % 8], i + t // 8)

            def three(dst, a_hi, a_lo, b_hi, b_lo, start, stop):
                first = nc.tensor.matmul(dst, a_hi, b_hi, start=start, stop=False)
                nc.tensor.matmul(dst, a_hi, b_lo, start=False, stop=False)
                return first, nc.tensor.matmul(dst, a_lo, b_hi, start=False, stop=stop)

            def weights(u, k, n, i=0, per=0):
                pe.wait_ge(unit_split, i * (2 * per) + 2 * (u + 1))
                return [w[:, u % 2, 0:k * n].rearrange("p (k n) -> p k n", k=k) for w in (w_hi, w_lo)]

            def unit_T(u, t, k, n, r_hi, r_lo, i=0, per=0, ready=None):
                hi, lo = weights(u, k, n, i, per)
                for c in range(n // P):
                    claim(t + c, i)
                    for kk in range(k):
                        if ready and c == 0:
                            ready(kk)
                        cc = slice(c * P, (c + 1) * P)
                        first, last = three(bank(t + c), hi[:, kk, cc], lo[:, kk, cc], r_hi[:, kk, :],
                                            r_lo[:, kk, :], kk == 0, kk == k - 1)
                        if c == 0 and kk == 0:
                            first.then_inc(unit_started, 1)
                    last.then_inc(psum_ready, 1)

            def unit_N(u, t, k, n, k0, start, stop, i=0, per=0):
                hi, lo = weights(u, k, n, i, per)
                for tt in range(NT):
                    if start:
                        claim(t + tt, i)
                    tok = slice(tt * P, (tt + 1) * P)
                    for kk in range(k):
                        first, last = three(ps[:, (t + tt) % 8, 0:n], hT_hi[:, k0 + kk, tok],
                                            hT_lo[:, k0 + kk, tok], hi[:, kk, :], lo[:, kk, :],
                                            start and kk == 0, stop and kk == k - 1)
                        if tt == 0 and kk == 0:
                            first.then_inc(unit_started, 1)
                    if stop:
                        last.then_inc(psum_ready, 1)

            def unit_L(u, t, k0, l_hi, l_lo, start, stop, ready):
                hi, lo = weights(u, 2, D)
                for kk in range(2):
                    ready(k0 + kk)
                for tt in range(NT):
                    tok = slice(tt * P, (tt + 1) * P)
                    for half in range(2):
                        if start:
                            claim(t + 2 * tt + half)
                        for kk in range(2):
                            cc = slice(half * 512, half * 512 + 512)
                            first, last = three(bank(t + 2 * tt + half), l_hi[:, k0 + kk, tok],
                                                l_lo[:, k0 + kk, tok], hi[:, kk, cc], lo[:, kk, cc],
                                                start and kk == 0, stop and kk == 1)
                            if tt == 0 and half == 0 and kk == 0:
                                first.then_inc(unit_started, 1)
                        if stop:
                            last.then_inc(psum_ready, 1)

            def long(phase, n, l_hi, l_lo, ready):
                for j in range(n):
                    unit_L(U0[phase] + j, T0[phase], 2 * j, l_hi, l_lo, j == 0, j == n - 1, ready)

            def transposes(t, blocks, width=P):
                claim(t)
                for n, src in enumerate(blocks):
                    k = src.shape[0]
                    last = nc.tensor.transpose(ps[:, t % 8, n * width:n * width + width], src, ident[0:k, 0:k])
                last.then_inc(psum_ready, 1)

            def h_transposes(phase, slot):
                for tt in range(NT):
                    h_in.take()
                    for half in range(2):
                        transposes(T0[phase] + 2 * tt + half,
                                   [slot[:, tt % 2, (4 * half + n) * P:(4 * half + n + 1) * P] for n in range(4)])

            def await_h(phase):
                for t in range(T0[phase], T0[phase] + 8):
                    await_evacuated(pe, t)

            def narrow(phase, r_hi, r_lo, ready=None):
                for j in range(4):
                    unit_T(U0[phase] + j, T0[phase] + 2 * j, KT, 256, r_hi, r_lo, ready=ready if j == 0 else None)

            def wide(phase, n=512):
                for h in range(2):
                    unit_N(U0[phase] + h, T0[phase], 4, n, 4 * h, h == 0, h == 1)

            pe.wait_ge(ident_loaded, 16)
            h_transposes("h1", slot1)
            pe.wait_ge(tables_loaded, 16 * 9)
            transposes(T0["conv_cols"], [conv_rows[:, n, :] for n in range(4)], 2 * FB)
            transposes(T0["spatial_T"], [spatial[:, g, :] for g in range(SGU_G)])
            await_h("h1")
            for b in range(2):
                for h in range(2):
                    unit_N(U0["qkvg"] + 2 * b + h, T0["qkvg"] + 4 * b, 4, 512, 4 * h, h == 0, h == 1)
            with pe.Fori(1, 3) as i:
                for b in range(2):
                    for h in range(2):
                        unit_N(U0["qkvg"] + 2 * b + h, T0["qkvg"] + 4 * b, 4, 512, 4 * h, h == 0, h == 1, i, 4)
            for tt in range(NT):
                for w in range(2):
                    pe.wait_ge(qk_rotated, 4 * w + tt + 1)
                    transposes(T0["qk_T"] + 2 * tt + w, [qk[:, w, tt, h * P:(h + 1) * P] for h in range(RET_H)])
            for t in range(T0["qk_T"], T0["qk_T"] + 8):
                await_evacuated(pe, t)
            t = T0["ret"]
            held = {}
            for kind, h in RETENTION:
                if kind == "scores":
                    for mb in range(NT):
                        claim(t)
                        nc.tensor.matmul(bank(t), kT[:, h, mb * P:(mb + 1) * P], qT[:, h, :],
                                         start=True, stop=True).then_inc(psum_ready, 1)
                        held[h, mb] = t
                        t += 1
                else:
                    for mb in range(NT):
                        await_evacuated(pe, held[h, mb])
                    for pair in range(2):
                        claim(t)
                        for nn in range(2):
                            n0 = (2 * pair + nn) * P
                            for mb in range(NT):
                                last = nc.tensor.matmul(ps[:, t % 8, nn * 256:nn * 256 + 256],
                                                        sT[:, h % 2, mb, n0:n0 + P],
                                                        v[:, mb, h * RET_DV:(h + 1) * RET_DV],
                                                        start=mb == 0, stop=mb == NT - 1)
                        last.then_inc(psum_ready, 1)
                        t += 1
            for b in range(2):
                for h in range(2):
                    unit_N(U0["sv"] + 2 * b + h, T0["sv"] + 4 * b, 4, 512, 4 * h, h == 0, h == 1)
            narrow("u", hT_hi, hT_lo)
            for tt in range(NT):
                pe.wait_ge(o_gated, tt + 1)
                for half in range(2):
                    transposes(T0["o_T"] + 2 * tt + half,
                               [o[:, tt, 2 * half + n // 2, n % 2 * P:n % 2 * P + P] for n in range(4)])
            pe.wait_ge(sv_normed, NT)
            for c in range(KT):
                t = T0["mix"] + c
                claim(t)
                for n in range(NT):
                    last = nc.tensor.matmul(ps[:, t % 8, n * P:(n + 1) * P], sv[:, n, c * P:(c + 1) * P],
                                            spatial_T[:, c // 2, :], start=True, stop=True)
                last.then_inc(psum_ready, 1)
            narrow("a_ret", hT_hi, hT_lo)
            await_h("o_T")
            narrow("y_ret", oT_hi, oT_lo)
            narrow("a_sgu", hT_hi, hT_lo)
            narrow("y_sgu", yT_hi, yT_lo, ready=lambda k: pe.wait_ge(lo_made, k + 1))
            long("out1", 4, mT_hi, mT_lo, ready=lambda k: pe.wait_ge(lo_made, KT + k + 1))
            h_transposes("h2", slot1)
            await_h("h2")
            t, u = T0["up1"], U0["up1"]
            with pe.Fori(0, FB // 4) as i:
                for j in range(4):
                    unit_T(u + j, t + 2 * j, KT, 256, hT_hi, hT_lo, i, 4)
            for j in range(FB // 4 * 4, FB):
                unit_T(u + j, t + 2 * j, KT, 256, hT_hi, hT_lo)
            long("down1", FB // 2, f_hi, f_lo, ready=lambda k: pe.wait_ge(f_made, k + 1))
            h_transposes("h3", slot2)
            await_h("h3")

            wide("kv_iq")
            wide("iq_ik", IB_W)
            wide("b_q")
            for tt in range(NT):
                pe.wait_ge(i_rotated, 3 * tt + 3)
                transposes(T0["i_T"] + tt, [kn[:, tt, 256:384], kn[:, tt, 384:512], ib[:, tt, 0:P], ib[:, tt, P:2 * P]])
            transposes(T0["i_T"] + 4, [ik2[:, tt, :, :].rearrange("p a d -> p (a d)") for tt in range(NT)])
            unit_N(U0["b_kv"], T0["b_kv"], KT, 256, 0, True, True)
            for t in range(T0["i_T"], T0["i_T"] + 5):
                await_evacuated(pe, t)
            t = T0["index"]
            for tt in range(1, NT):
                n = (tt + 1) * P
                for h in range(HEADS):
                    claim(t)
                    r = slice(HD * (h % 2), HD * (h % 2) + HD)
                    nc.tensor.matmul(ps[:, t % 8, 0:n], qT_a[r, h // 2, tt * P:(tt + 1) * P], ikT[r, 0:n],
                                     start=True, stop=True).then_inc(psum_ready, 1)
                    t += 1
            narrow("g_b", hT_hi, hT_lo)
            narrow("g_a", hT_hi, hT_lo)

            def head_pairs(src, tt, t):
                transposes(t, [src[:, tt, r * P:(r + 1) * P] for r in range(4)])

            for tt in range(NT):
                pe.wait_ge(b_rotated, 2 * tt + 2)
                head_pairs(qn, tt, T0["b_T"] + tt)
            transposes(T0["b_T"] + 4, [bkv[:, tt, 0:P] for tt in range(NT)])
            wide("a_q")

            def attention(base, q, k, val, first_key, made, outs):
                t = base
                held = {}
                for kind, s in ATTENTION:
                    tt, h = (s // HEADS, s % HEADS) if kind != "out_T" else (s, 0)
                    r = slice(HD * (h // 4), HD * (h // 4) + HD)
                    k0 = first_key(tt)
                    nk = tt + 1 - k0
                    claim(t)
                    held[kind, s] = t
                    if kind == "logits":
                        nc.tensor.matmul(ps[:, t % 8, 0:nk * P], q[r, h % 4, tt * P:(tt + 1) * P],
                                         k[r, k0 * P:(tt + 1) * P], start=True, stop=True).then_inc(psum_ready, 1)
                    elif kind == "probs_T":
                        pe.wait_ge(probs_made, outs * 32 + s + 1)
                        for n in range(nk):
                            last = nc.tensor.transpose(ps[:, t % 8, n * P:(n + 1) * P],
                                                       probs[:, s % 4, n * P:(n + 1) * P], ident[:, :])
                        last.then_inc(psum_ready, 1)
                    elif kind == "values":
                        await_evacuated(pe, held["probs_T", s])
                        for n in range(nk):
                            last = nc.tensor.matmul(ps[:, t % 8, 0:HD], probs_T[:, s % 2, n * P:(n + 1) * P],
                                                    val(k0 + n, h // 4), start=n == 0, stop=n == nk - 1)
                        last.then_inc(psum_ready, 1)
                    else:
                        pe.wait_ge(o2_made, outs * NT + tt + 1)
                        for n in range(4):
                            last = nc.tensor.transpose(ps[:, t % 8, n * P:(n + 1) * P],
                                                       o2[:, tt % 2, n * P:(n + 1) * P], ident[:, :])
                        last.then_inc(psum_ready, 1)
                    t += 1
                return [held["out_T", tt] for tt in range(NT)]

            for t in range(T0["b_T"], T0["b_T"] + 5):
                await_evacuated(pe, t)
            for t in attention(T0["swa"], qT_b, bkT, lambda kb, g: bkv[:, kb, P + g * HD:P + (g + 1) * HD],
                               lambda tt: max(tt - 1, 0), probs_made, 0):
                await_evacuated(pe, t)
            for j in range(2):
                unit_T(U0["y_b"] + j, T0["y_b"] + 4 * j, 4, 512, oTb_hi, oTb_lo)
            for tt in range(NT):
                pe.wait_ge(a_rotated, 2 * tt + 2)
                head_pairs(qn, tt, T0["a_T"] + tt)
            transposes(T0["a_T"] + 4, [kn[:, tt, 0:P] for tt in range(NT)])
            for t in range(T0["a_T"], T0["a_T"] + 5):
                await_evacuated(pe, t)
            for t in attention(T0["dsa"], qT_a, akT, lambda kb, g: kn[:, kb, P + g * HD:P + (g + 1) * HD],
                               lambda tt: 0, probs_made, 1):
                await_evacuated(pe, t)
            for j in range(2):
                unit_T(U0["y_a"] + j, T0["y_a"] + 4 * j, 4, 512, oTa_hi, oTa_lo)
            long("out2", 4, m2_hi, m2_lo, ready=lambda k: pe.wait_ge(lo_made, 2 * KT + k + 1))
            h_transposes("h4", slot3)
            await_h("h4")
            for half in range(2):
                t, u = T0[f"up2_{half}"], U0[f"up2_{half}"]
                with pe.Fori(0, 2) as i:
                    for j in range(4):
                        unit_T(u + j, t + 2 * j, KT, 256, hT_hi, hT_lo, i, 4)
                long(f"down2_{half}", 8, f2_hi, f2_lo,
                     ready=lambda k, half=half: pe.wait_ge(f2_made, 16 * half + k + 1))

        STEPS = [("A", 0), ("A", 1), ("B", 0), ("C", 0), ("A", 2), ("B", 1), ("C", 1), ("A", 3),
                 ("B", 2), ("C", 2), ("B", 3), ("C", 3)]

        @block.scalar
        def _(act):
            step = Count(act, act_step)
            rms_out = Count(act, rms_made)
            x_in = Count(act, x_updated)
            hi_out = Count(act, hi_made)
            hot_in = Count(act, hot)

            def evacuate(t, dst, func, src=None):
                await_psum(act, t)
                nc.scalar.activation(dst, bank(t) if src is None else src, func).then_inc(evacuated[t % 8], 1)

            def load_gain(n, src):
                act.dma_start(gain[:, n, :], src.partition_broadcast(P)).then_inc(gains_loaded, 16)

            def boundary(kind, tin, tout, slot):
                for which, tt in STEPS:
                    junk = slot[:, tt % 2, :]
                    if tt >= 2 and which == ("A" if kind == "norm" else "B"):
                        if tout is not None:
                            await_psum(act, tout + 2 * (tt - 2) + 1)
                        else:
                            act.wait_ge(stored[tt % 2], 16)
                    rms_out.wait()
                    if which == "A" and kind == "norm":
                        await_psum(act, tin + 2 * tt + 1)
                        for half in range(2):
                            step.up(nc.scalar.activation(junk[:, half * 512:half * 512 + 512],
                                                         bank(tin + 2 * tt + half), ACT.Square,
                                                         accum_out=sq[:, half:half + 1]))
                        step.wait()
                        step.up(nc.scalar.activation(sq[:, 2:3], sq[:, 1:2], ACT.Identity, bias=eps, scale=1.0 / D))
                        step.wait()
                        rms_out.up(nc.scalar.activation(rms[:, 2 * tt:2 * tt + 1], sq[:, 0:1], ACT.Sqrt,
                                                        bias=sq[:, 2:3], scale=1.0 / D))
                    elif which == "B":
                        if kind == "none":
                            act.wait_ge(x_loaded[tt], 16)
                        elif kind == "plain":
                            for half in range(2):
                                await_evacuated(act, tin + 2 * tt + half)
                        else:
                            x_in.take()
                        step.up(nc.scalar.activation(junk, x[:, tt, :], ACT.Square, accum_out=sq[:, 3:4]))
                        step.wait()
                        rms_out.up(nc.scalar.activation(rms[:, 2 * tt + 1:2 * tt + 2], sq[:, 3:4], ACT.Sqrt,
                                                        bias=eps, scale=1.0 / D))
                    elif which == "C" and tout is not None:
                        for half in range(2):
                            t = tout + 2 * tt + half
                            await_psum(act, t)
                            hi_out.up(nc.scalar.activation(
                                hT_hi[:, 4 * half:4 * half + 4, tt * P:(tt + 1) * P],
                                bank(t).rearrange("p (k n) -> p k n", k=4), ACT.Copy))

            act.wait_ge(eps_set, 1)
            boundary("none", None, T0["h1"], slot1)
            evacuate(T0["conv_cols"], conv[:, :, :], ACT.Copy,
                     ps[:, T0["conv_cols"] % 8, 0:8 * FB].rearrange("p (t j) -> p t j", t=4))
            evacuate(T0["spatial_T"], spatial_T[:, :, :], ACT.Copy,
                     bank(T0["spatial_T"]).rearrange("p (g q) -> p g q", g=SGU_G))
            act.wait_ge(gamma_arg, 1)
            nc.scalar.activation(gm[2], gm[1], ACT.Exp).then_inc(gamma_exp, 1)

            def decay_exp(h):
                act.wait_ge(decay_arg, h + 1)
                nc.scalar.activation(decay[:, h % 2, :], decay[:, h % 2, :], ACT.Exp).then_inc(decay_made, 1)

            decay_exp(0)
            decay_exp(1)
            await_evacuated(act, T0["h1"] + 7)
            load_gain(0, a["sgu_ln_g"])
            load_gain(1, a["sgu_ln_b"])
            for b in range(2):
                for tt in range(NT):
                    evacuate(T0["qkvg"] + 8 + 4 * b + tt, v[:, tt, b * 512:b * 512 + 512], ACT.Copy)
            for b in range(2):
                for tt in range(NT):
                    evacuate(T0["qkvg"] + 16 + 4 * b + tt, silu_g[:, tt, b * 512:b * 512 + 512], ACT.Silu)
            for tt in range(NT):
                for w, dst in ((0, qT), (1, kT)):
                    t = T0["qk_T"] + 2 * tt + w
                    evacuate(t, dst[:, :, tt * P:(tt + 1) * P], ACT.Copy,
                             bank(t).rearrange("p (h n) -> p h n", h=RET_H))
            t = T0["ret"]
            for kind, h in RETENTION:
                if kind == "scores":
                    t += NT
                    continue
                if h + 2 < RET_H:
                    decay_exp(h + 2)
                for pair in range(2):
                    evacuate(t, o[:, 2 * pair:2 * pair + 2, h, :], ACT.Copy,
                             bank(t).rearrange("p (n e) -> p n e", n=2))
                    t += 1
            act.wait_ge(o_stats, NT * RET_H)
            nc.scalar.activation(o_stat[:, 60:76], o_stat[:, 13:45:2], ACT.Sqrt, bias=eps).then_inc(o_rms, 1)
            for b in range(2):
                for tt in range(NT):
                    evacuate(T0["sv"] + 4 * b + tt, sv[:, tt, b * 512:b * 512 + 512], ACT.Gelu_apprx_tanh)
            await_evacuated(act, T0["ret"] + 19)
            act.dma_start(spatial_b[:, :, :].rearrange("p g q -> p (g q)"),
                          a["b_spatial"].rearrange("g q -> (g q)").partition_broadcast(P)).then_inc(spatial_b_loaded, 16)
            act.wait_ge(sv_stats, NT)
            nc.scalar.activation(sv_stat[:, 64:68], sv_stat[:, 49:57:2], ACT.Sqrt, bias=eps).then_inc(sv_rms, 1)
            for c in range(KT):
                evacuate(T0["u"] + c, uT[:, c, :], ACT.Gelu_apprx_tanh)
            for tt in range(NT):
                for half in range(2):
                    t = T0["o_T"] + 2 * tt + half
                    await_psum(act, t)
                    hi_out.up(nc.scalar.activation(oT_hi[:, 4 * half:4 * half + 4, tt * P:(tt + 1) * P],
                                                   bank(t).rearrange("p (k n) -> p k n", k=4), ACT.Copy))
            for c in range(KT):
                hot_in.take()
                hi_out.up(nc.scalar.activation(yT_hi[:, c, :], uT[:, c, :], ACT.Copy))
            act.wait_ge(sv_normed, NT)
            load_gain(0, a["g_post_mix"])
            load_gain(1, a["g_pre_ffn"])
            for c in range(KT):
                evacuate(T0["a_ret"] + c, mT[:, c, :], ACT.Sigmoid)
            for c in range(KT):
                evacuate(T0["a_sgu"] + c, sgu_gate[:, c, :], ACT.Sigmoid)
            for c in range(KT):
                hot_in.take()
                hi_out.up(nc.scalar.activation(mT_hi[:, c, :], mT[:, c, :], ACT.Copy))
            boundary("norm", T0["out1"], T0["h2"], slot1)
            await_evacuated(act, T0["h2"] + 7)
            load_gain(0, a["g_post_ffn"])
            load_gain(1, a["attn_norm"])

            def up_unit(j, i=0):
                t = T0["up1"] + 2 * j
                if j >= 2 or not isinstance(i, int):
                    act.wait_ge(f_made, i * 4 + (j - 1))
                for c in range(2):
                    await_psum(act, t + c, i)
                    col = i * 4 + (j + c * FB)
                    nc.scalar.activation(taps[:, j % 2, c, :], bank(t + c), ACT.Identity,
                                         bias=conv[:, 3, bass.ds(col, 1)],
                                         scale=conv[:, 1, bass.ds(col, 1)]).then_inc(centre, 1)
                await_evacuated(act, t, i)
                nc.scalar.activation(taps[:, j % 2, 0, :], taps[:, j % 2, 0, :],
                                     ACT.Gelu_apprx_tanh).then_inc(gelu_made, 1)
                act.wait_ge(gated, i * 4 + (j + 1))
                nc.scalar.activation(f_hi[:, bass.ds(i * 4 + j, 1), :], taps[:, j % 2, 0:1, :],
                                     ACT.Copy).then_inc(f_hi_made, 1)

            for j in range(4):
                up_unit(j)
            with act.Fori(1, FB // 4) as i:
                for j in range(4):
                    up_unit(j, i)
            for j in range(FB // 4 * 4, FB):
                up_unit(j)
            boundary("norm", T0["down1"], T0["h3"], slot2)

            for n, name in enumerate(("ik_norm_w", "ik_norm_b")):
                act.dma_start(ik_gain[:, n, :], a[name].partition_broadcast(P)).then_inc(ik_gain_loaded, 16)

            for tt in range(NT):
                evacuate(T0["kv_iq"] + tt, kn[:, tt, :], ACT.Copy)
            for tt in range(NT):
                t = T0["iq_ik"] + tt
                evacuate(t, ib[:, tt, :], ACT.Copy, ps[:, t % 8, 0:IB_W])
            act.wait_ge(ik_stats, NT)
            nc.scalar.activation(ik_stat[:, 40:44], ik_stat[:, 25:33:2], ACT.Sqrt, bias=eps).then_inc(ik_rms, 1)

            def evacuate_pairs(t, dst):
                evacuate(t, dst.rearrange("p (r g d) -> p g r d", r=4, g=2), ACT.Copy,
                         bank(t).rearrange("p (g r d) -> p g r d", g=2, r=4))

            for tt in range(NT):
                evacuate_pairs(T0["b_q"] + tt, qn[:, tt, :])

            def evacuate_T(base, dst):
                for tt in range(NT):
                    evacuate(base + tt, dst[:, :, tt * P:(tt + 1) * P], ACT.Copy,
                             bank(base + tt).rearrange("p (r n) -> p r n", r=4))

            evacuate_T(T0["i_T"], qT_a)
            evacuate(T0["i_T"] + 4, ikT[:, :], ACT.Copy)
            for tt in range(NT):
                t = T0["b_kv"] + tt
                evacuate(t, bkv[:, tt, :], ACT.Copy, ps[:, t % 8, 0:2 * P])
            t = T0["index"]
            for s in range((NT - 1) * HEADS):
                n = (s // HEADS + 2) * P
                await_psum(act, t + s)
                if s >= 2:
                    act.wait_ge(hot, 2 * KT + s - 1)
                nc.scalar.activation(relu[:, s % 2, 0:n], ps[:, (t + s) % 8, 0:n],
                                     ACT.Relu).then_inc(evacuated[(t + s) % 8], 1)
            for c in range(KT):
                evacuate(T0["g_b"] + c, sig_b[:, c, :], ACT.Sigmoid)
            for c in range(KT):
                evacuate(T0["g_a"] + c, sig_a[:, c, :], ACT.Sigmoid)
            evacuate_T(T0["b_T"], qT_b)
            evacuate(T0["b_T"] + 4, bkT[:, :], ACT.Copy)
            for tt in range(NT):
                evacuate_pairs(T0["a_q"] + tt, qn[:, tt, :])

            def attention(base, first_key, hi, branch):
                for n, (kind, s) in enumerate(ATTENTION):
                    t = base + n
                    if kind == "logits":
                        tt, h = s // HEADS, s % HEADS
                        nk = tt + 1 - first_key(tt)
                        if h == 0 and (tt >= 2 or branch):
                            act.wait_ge(o2_made, NT * branch + tt - 1)
                        await_evacuated(act, t)
                        nc.scalar.activation(probs[:, s % 4, 0:nk * P], probs[:, s % 4, 0:nk * P], ACT.Exp,
                                             bias=nm[:, tt % 2, h:h + 1], scale=-1.0,
                                             accum_out=rs[:, tt % 2, h:h + 1]).then_inc(probs_made, 1)
                    elif kind == "values":
                        tt, h = s // HEADS, s % HEADS
                        if h == HEADS - 1 and branch == 0:
                            act.wait_ge(sinks_arg, tt + 1)
                            nc.scalar.activation(sink_e[:, tt % 2, :], sink_e[:, tt % 2, :],
                                                 ACT.Exp).then_inc(sinks_exp, 1)
                        if h == 0 and tt >= 2:
                            await_psum(act, base + ATTENTION.index(("out_T", tt - 2)))
                        await_psum(act, t)
                        nc.scalar.activation(o2[:, tt % 2, h * HD:(h + 1) * HD], ps[:, t % 8, 0:HD],
                                             ACT.Copy).then_inc(evacuated[t % 8], 1)
                    elif kind == "out_T":
                        await_psum(act, t)
                        hi_out.up(nc.scalar.activation(hi[:, :, s * P:(s + 1) * P],
                                                       bank(t).rearrange("p (k n) -> p k n", k=4), ACT.Copy))

            attention(T0["swa"], lambda tt: max(tt - 1, 0), oTb_hi, 0)
            evacuate_T(T0["a_T"], qT_a)
            evacuate(T0["a_T"] + 4, akT[:, :], ACT.Copy)
            attention(T0["dsa"], lambda tt: 0, oTa_hi, 1)
            await_evacuated(act, T0["dsa"] + ATTENTION.index(("logits", NT * HEADS - 1)))
            load_gain(0, a["mlp_norm"])
            load_gain(1, a["final_norm"])
            hot_in.n += (NT - 1) * HEADS
            for c in range(KT):
                hot_in.take()
                hi_out.up(nc.scalar.activation(m2_hi[:, c, :], sig_a[:, c, :], ACT.Copy))
            boundary("plain", T0["out2"], T0["h4"], slot3)
            for half in range(2):
                with act.Fori(0, 2) as i:
                    for j in range(8):
                        t = T0[f"up2_{half}"] + j
                        await_evacuated(act, t, i)
                        nc.scalar.activation(f2_t[:, j % 4, :], f2_t[:, j % 4, :], ACT.Square).then_inc(squared, 1)
                        act.wait_ge(squared, i * 8 + (16 * half + j + 1))
                        nc.scalar.activation(f2_hi[:, bass.ds(i * 8 + j, 1), :], f2_t[:, j % 4:j % 4 + 1, :],
                                             ACT.Copy).then_inc(f2_hi_made, 1)
            boundary("plain", T0["down2_1"], None, slot4)

        @block.vector
        def _(dve):
            step = Count(dve, dve_step)
            rms_in = Count(dve, rms_made)
            x_out = Count(dve, x_updated)
            h_out = Count(dve, h_made)
            hi_in = Count(dve, hi_made)
            hot_out = Count(dve, hot)
            lo_out = Count(dve, lo_made)
            V = nc.vector

            def boundary(kind, tin, tout, slot, post, pre):
                for which, tt in STEPS:
                    c = 2 * tt + (which == "B")
                    if which == "A" and kind == "norm":
                        rms_in.take()
                        step.up(V.reciprocal(rstd[:, c:c + 1], rms[:, c:c + 1]))
                        step.wait()
                        for half in range(2):
                            t = tin + 2 * tt + half
                            cc = slice(half * 512, half * 512 + 512)
                            V.scalar_tensor_tensor(slot[:, tt % 2, cc], bank(t), rstd[:, c:c + 1], gain[:, post, cc],
                                                   ALU.mult, ALU.mult).then_inc(evacuated[t % 8], 1)
                        for half in range(2):
                            await_evacuated(dve, tin + 2 * tt + half)
                        x_out.up(V.tensor_tensor(x[:, tt, :], x[:, tt, :], slot[:, tt % 2, :], ALU.add))
                    elif which == "A" and kind == "plain":
                        for half in range(2):
                            t = tin + 2 * tt + half
                            cc = slice(half * 512, half * 512 + 512)
                            await_psum(dve, t)
                            V.tensor_tensor(x[:, tt, cc], bank(t), x[:, tt, cc], ALU.add).then_inc(evacuated[t % 8], 1)
                    elif which == "B":
                        rms_in.take()
                        if kind == "none":
                            dve.wait_ge(x_loaded[tt], 16)
                        elif kind == "plain":
                            for half in range(2):
                                await_evacuated(dve, tin + 2 * tt + half)
                        step.up(V.reciprocal(rstd[:, c:c + 1], rms[:, c:c + 1]))
                        step.wait()
                        made = V.scalar_tensor_tensor(slot[:, tt % 2, :], x[:, tt, :], rstd[:, c:c + 1], gain[:, pre, :],
                                                      ALU.mult, ALU.mult)
                        if tout is None:
                            made.then_inc(out_made, 1)
                        else:
                            h_out.up(made)
                    elif which == "C" and tout is not None:
                        for half in range(2):
                            t = tout + 2 * tt + half
                            dst = (slice(None), slice(4 * half, 4 * half + 4), slice(tt * P, (tt + 1) * P))
                            hi_in.take()
                            V.tensor_tensor(hT_lo[dst], bank(t).rearrange("p (k n) -> p k n", k=4),
                                            hT_hi[dst].bitcast(f32), ALU.subtract).then_inc(evacuated[t % 8], 1)

            V.memset(eps, EPS).then_inc(eps_set, 1)
            dve.wait_ge(gains_loaded, 16)
            boundary("none", None, T0["h1"], slot1, None, 0)

            dve.wait_ge(tables_loaded, 16 * 9)
            step.up(V.tensor_scalar(gm[0], lg, -1.0, None, ALU.mult))
            step.up(V.tensor_scalar(nsink, sink, -1.0, None, ALU.mult))
            step.wait()
            V.tensor_tensor(gm[1], gm[0], lg, ALU.min).then_inc(gamma_arg, 1)
            dve.wait_ge(gamma_exp, 1)
            step.up(V.tensor_scalar(gm[3], gm[2], 2.0, None, ALU.add))
            step.wait()
            step.up(V.reciprocal(gm[4], gm[3]))
            step.wait()
            step.up(V.tensor_tensor(gm[3], gm[2], gm[4], ALU.mult))
            step.wait()
            step.up(V.tensor_tensor(gm[4], gm[3], gm[3], ALU.mult))
            step.wait()
            step.up(V.tensor_scalar(gm[5], gm[4], 1.0 / 17, None, ALU.mult))
            for odd in range(15, 1, -2):
                step.wait()
                step.up(V.scalar_tensor_tensor(gm[5], gm[5], 1.0 / odd, gm[4], ALU.add, ALU.mult))
            step.wait()
            step.up(V.scalar_tensor_tensor(gm[6], gm[5], 1.0, gm[3], ALU.add, ALU.mult))
            step.up(V.tensor_scalar(gm[7], lg, 0.0, None, ALU.min))
            step.wait()
            step.up(V.scalar_tensor_tensor(lg, gm[6], -2.0, gm[7], ALU.mult, ALU.add))
            step.wait()
            step.up(V.tensor_scalar(gm[0], lg, -1.0, None, ALU.mult))

            rotated = {name: Count(dve, s) for name, s in (("qk", qk_rotated), ("i", i_rotated),
                                                           ("b", b_rotated), ("a", a_rotated))}
            last_rope = [step]

            def rope(src, dst, heads, half, table, tt, tmp, tile_of, count):
                n = heads * 2 * half
                view = [P, heads, 2, half]
                c = table[:, tt, 0, None, None, :].broadcast_to(view)
                s = table[:, tt, None, 1:3, :].broadcast_to(view)
                ta, tb = [tmp[:, k, 0:n].rearrange("p (h a d) -> p h a d", h=heads, a=2) for k in range(2)]
                t4 = src.rearrange("p (h a d) -> p h a d", h=heads, a=2)
                last_rope[0].wait()
                last_rope[0] = count
                step.up(V.tensor_tensor(ta, t4, c, ALU.mult))
                last = V.tensor_tensor(tb, t4[:, :, ::-1, :], s, ALU.mult)
                if tile_of is None:
                    step.up(last)
                else:
                    last.then_inc(evacuated[tile_of % 8], 1)
                    await_evacuated(dve, tile_of)
                step.wait()
                count.up(V.tensor_tensor(dst, tmp[:, 0, 0:n], tmp[:, 1, 0:n], ALU.add))

            for w in range(2):
                for tt in range(NT):
                    t = T0["qkvg"] + 4 * w + tt
                    await_psum(dve, t)
                    rope(bank(t), qk[:, w, tt, :], RET_H, RET_DK // 2, rope1, tt, rope_t, t, rotated["qk"])

            def decay_args(h):
                if h:
                    dve.wait_ge(decay_arg, h)
                step.up(V.tensor_scalar(decay[:, h % 2, :], distance[:, :], 0.0, lg[:, h:h + 1], ALU.max, ALU.mult))
                step.up(V.tensor_scalar(decay[:, 2, :], distance[:, :], 0.0, gm[0][:, 4 + h:5 + h], ALU.min, ALU.mult))
                step.wait()
                V.tensor_tensor(decay[:, h % 2, :], decay[:, h % 2, :], decay[:, 2, :], ALU.add).then_inc(decay_arg, 1)

            decay_args(0)
            decay_args(1)
            t = T0["ret"]
            for kind, h in RETENTION:
                if kind == "scores":
                    dve.wait_ge(decay_made, h + 1)
                    for mb in range(NT):
                        if h >= 2 and mb == 0:
                            await_psum(dve, t - 1)
                        await_psum(dve, t)
                        V.scalar_tensor_tensor(sT[:, h % 2, mb, :], bank(t), RET_DK ** -0.5,
                                               decay[:, h % 2, (NT - 1 - mb) * P:(NT - 1 - mb) * P + S],
                                               ALU.mult, ALU.mult).then_inc(evacuated[t % 8], 1)
                        t += 1
                    if h + 2 < RET_H:
                        for b in range(t - NT, t):
                            await_evacuated(dve, b)
                        decay_args(h + 2)
                else:
                    for pair in range(2):
                        await_evacuated(dve, t)
                        for nn in range(2):
                            at_ = h * NT + 2 * pair + nn
                            if at_ == 0:
                                await_evacuated(dve, T0["ret"] + 2 * NT - 1)
                            else:
                                dve.wait_ge(o_stats, at_)
                            six = o_stat[:, 6 * (at_ % 2):6 * (at_ % 2) + 6]
                            step.up(V.bn_stats(six, o[:, 2 * pair + nn, h, :]))
                            step.wait()
                            V.bn_aggr(o_stat[:, 12 + 2 * at_:14 + 2 * at_], six).then_inc(o_stats, 1)
                        t += 1
            dve.wait_ge(o_rms, 1)
            step.up(V.reciprocal(o_stat[:, 44:60], o_stat[:, 60:76]))
            step.wait()
            for tt in range(NT):
                for h in range(RET_H):
                    n = h * NT + tt
                    step.up(V.tensor_scalar(o[:, tt, h, :], o[:, tt, h, :], o_stat[:, 12 + 2 * n:13 + 2 * n],
                                            o_stat[:, 44 + n:45 + n], ALU.subtract, ALU.mult))
                step.wait()
                row = o[:, tt, :, :].rearrange("p h e -> p (h e)")
                V.tensor_tensor(row, row, silu_g[:, tt, :], ALU.mult).then_inc(o_gated, 1)

            for tt in range(NT):
                for b in range(2):
                    await_evacuated(dve, T0["sv"] + 4 * b + tt)
                    step.up(V.bn_stats(sv_stat[:, 12 * tt + 6 * b:12 * tt + 6 * b + 6], sv[:, tt, b * 512:b * 512 + 512]))
                step.wait()
                V.bn_aggr(sv_stat[:, 48 + 2 * tt:50 + 2 * tt],
                          sv_stat[:, 12 * tt:12 * tt + 12]).then_inc(sv_stats, 1)
            dve.wait_ge(sv_rms, 1)
            step.up(V.reciprocal(sv_stat[:, 68:72], sv_stat[:, 64:68]))
            step.wait()
            dve.wait_ge(gains_loaded, 16 * 3)
            for tt in range(NT):
                step.up(V.tensor_scalar(sv[:, tt, :], sv[:, tt, :], sv_stat[:, 48 + 2 * tt:49 + 2 * tt],
                                        sv_stat[:, 68 + tt:69 + tt], ALU.subtract, ALU.mult))
                step.wait()
                step.up(V.tensor_tensor(sv[:, tt, :], sv[:, tt, :], gain[:, 0, :], ALU.mult))
                step.wait()
                V.tensor_tensor(sv[:, tt, :], sv[:, tt, :], gain[:, 1, :], ALU.add).then_inc(sv_normed, 1)
            for tt in range(NT):
                for half in range(2):
                    t = T0["o_T"] + 2 * tt + half
                    dst = (slice(None), slice(4 * half, 4 * half + 4), slice(tt * P, (tt + 1) * P))
                    hi_in.take()
                    V.tensor_tensor(oT_lo[dst], bank(t).rearrange("p (k n) -> p k n", k=4),
                                    oT_hi[dst].bitcast(f32), ALU.subtract).then_inc(evacuated[t % 8], 1)

            def y_low(c):
                hi_in.take()
                lo_out.up(V.tensor_tensor(yT_lo[:, c, :], uT[:, c, :], yT_hi[:, c, :].bitcast(f32), ALU.subtract))

            dve.wait_ge(spatial_b_loaded, 16)
            for c in range(KT):
                t = T0["mix"] + c
                await_psum(dve, t)
                V.tensor_tensor(mix_t[:, c % 2, :].rearrange("p (n q) -> p n q", n=NT),
                                bank(t).rearrange("p (n q) -> p n q", n=NT),
                                spatial_b[:, None, c // 2, :].broadcast_to([P, NT, P]),
                                ALU.add).then_inc(evacuated[t % 8], 1)
                await_evacuated(dve, t)
                await_evacuated(dve, T0["u"] + c)
                hot_out.up(V.tensor_tensor(uT[:, c, :], mix_t[:, c % 2, :], uT[:, c, :], ALU.mult))
                if c:
                    y_low(c - 1)
            y_low(KT - 1)

            def gate(base, gates, g_base):
                for c in range(KT):
                    await_psum(dve, base + c)
                    await_evacuated(dve, g_base + c)
                    V.tensor_tensor(gates[:, c, :], bank(base + c), gates[:, c, :],
                                    ALU.mult).then_inc(evacuated[(base + c) % 8], 1)

            def gate_and_merge(base, gates, other, merged, g_base, hi, lo, other_base):
                def low(c):
                    hi_in.take()
                    lo_out.up(V.tensor_tensor(lo[:, c, :], merged[:, c, :], hi[:, c, :].bitcast(f32), ALU.subtract))

                for c in range(KT):
                    await_psum(dve, base + c)
                    await_evacuated(dve, g_base + c)
                    V.tensor_tensor(gates[:, c, :], bank(base + c), gates[:, c, :],
                                    ALU.mult).then_inc(evacuated[(base + c) % 8], 1)
                    await_evacuated(dve, base + c)
                    await_evacuated(dve, other_base + c)
                    hot_out.up(V.tensor_tensor(merged[:, c, :], gates[:, c, :], other[:, c, :], ALU.add))
                    if c:
                        low(c - 1)
                low(KT - 1)

            gate(T0["y_ret"], mT, T0["a_ret"])
            gate_and_merge(T0["y_sgu"], sgu_gate, mT, mT, T0["a_sgu"], mT_hi, mT_lo, T0["y_ret"])
            dve.wait_ge(gains_loaded, 16 * 5)
            boundary("norm", T0["out1"], T0["h2"], slot1, 0, 1)

            def up_unit(j, i=0):
                t = T0["up1"] + 2 * j
                for c in range(2):
                    tap = taps[:, j % 2, c, :]
                    col = i * 4 + (j + c * FB)
                    dve.wait_ge(centre, i * 8 + (2 * j + c + 1))
                    V.scalar_tensor_tensor(tap[:, 1:S], ps[:, (t + c) % 8, 0:S - 1], conv[:, 0, bass.ds(col, 1)],
                                           tap[:, 1:S], ALU.mult, ALU.add).then_inc(left, 1)
                    dve.wait_ge(left, i * 8 + (2 * j + c + 1))
                    V.scalar_tensor_tensor(tap[:, 0:S - 1], ps[:, (t + c) % 8, 1:S], conv[:, 2, bass.ds(col, 1)],
                                           tap[:, 0:S - 1], ALU.mult, ALU.add).then_inc(evacuated[(t + c) % 8], 1)
                dve.wait_ge(gelu_made, i * 4 + (j + 1))
                await_evacuated(dve, t + 1, i)
                V.tensor_tensor(taps[:, j % 2, 0, :], taps[:, j % 2, 0, :], taps[:, j % 2, 1, :],
                                ALU.mult).then_inc(gated, 1)
                dve.wait_ge(f_hi_made, i * 4 + (j + 1))
                at_ = bass.ds(i * 4 + j, 1)
                V.tensor_tensor(f_lo[:, at_, :], taps[:, j % 2, 0:1, :], f_hi[:, at_, :].bitcast(f32),
                                ALU.subtract).then_inc(f_made, 1)

            with dve.Fori(0, FB // 4) as i:
                for j in range(4):
                    up_unit(j, i)
            for j in range(FB // 4 * 4, FB):
                up_unit(j)
            dve.wait_ge(gains_loaded, 16 * 7)
            boundary("norm", T0["down1"], T0["h3"], slot2, 0, 1)

            for tt in range(NT):
                await_evacuated(dve, T0["iq_ik"] + tt)
                step.up(V.bn_stats(ik_stat[:, 6 * tt:6 * tt + 6], ib[:, tt, 256:256 + HD]))
                step.wait()
                V.bn_aggr(ik_stat[:, 24 + 2 * tt:26 + 2 * tt], ik_stat[:, 6 * tt:6 * tt + 6]).then_inc(ik_stats, 1)
            dve.wait_ge(ik_rms, 1)
            step.up(V.reciprocal(ik_stat[:, 44:48], ik_stat[:, 40:44]))
            step.wait()
            for tt in range(NT):
                key = ib[:, tt, 256:256 + HD]
                step.up(V.tensor_scalar(key, key, ik_stat[:, 24 + 2 * tt:25 + 2 * tt], ik_stat[:, 44 + tt:45 + tt],
                                        ALU.subtract, ALU.mult))
                step.wait()
                if tt == 0:
                    dve.wait_ge(ik_gain_loaded, 32)
                step.up(V.tensor_tensor(key, key, ik_gain[:, 0, :], ALU.mult))
                step.wait()
                step.up(V.tensor_tensor(key, key, ik_gain[:, 1, :], ALU.add))
                step.wait()
                rope(key, ik2[:, tt, 0, :], 1, HD // 2, rope2, tt, rope_u, None, step)
                step.wait()
                rope(kn[:, tt, 256:512], kn[:, tt, 256:512], 4, HD // 2, rope2, tt, rope_u, None, rotated["i"])
                rope(ib[:, tt, 0:256], ib[:, tt, 0:256], 4, HD // 2, rope2, tt, rope_u, None, rotated["i"])
                rotated["i"].up(V.tensor_copy(ik2[:, tt, 1, :], ik2[:, tt, 0, :]))
                w8 = ib[:, tt, 256 + HD:256 + HD + HEADS]
                step.up(V.tensor_scalar(w8, w8, HEADS ** -0.5 * HD ** -0.5, None, ALU.mult))
            step.wait()

            step.up(V.tensor_copy(mask[:, 0, 0:P], band[:, P:2 * P]))
            for tt in range(1, NT):
                n = (tt + 1) * P
                for h in range(HEADS):
                    s = (tt - 1) * HEADS + h
                    t = T0["index"] + s
                    await_evacuated(dve, t)
                    w = ib[:, tt, 256 + HD + h:257 + HD + h]
                    if h == 0:
                        hot_out.up(V.tensor_scalar(score[:, 0:n], relu[:, s % 2, 0:n], w, None, ALU.mult))
                    else:
                        hot_out.wait()
                        hot_out.up(V.scalar_tensor_tensor(score[:, 0:n], relu[:, s % 2, 0:n], w, score[:, 0:n],
                                                          ALU.mult, ALU.add))
                hot_out.wait()
                step.up(V.tensor_tensor(score[:, tt * P:n], score[:, tt * P:n], band[:, P:2 * P], ALU.add))
                for r in range(TOPK // 8):
                    src = score if r == 0 else work
                    step.wait()
                    step.up(V.max(top[:, 0:8], src[:, 0:n]))
                    step.wait()
                    if r < TOPK // 8 - 1:
                        step.up(V.match_replace(work[:, 0:n], top[:, 0:8], src[:, 0:n], LOWEST))
                kth = top[:, 7:8]
                step.up(V.tensor_scalar(above[:, 0:n], score[:, 0:n], kth, 0.0, ALU.is_gt, ALU.add,
                                        accum_out=top[:, 8:9]))
                step.up(V.tensor_scalar(equal[:, 0:n], score[:, 0:n], kth, None, ALU.is_equal))
                step.wait()
                step.up(V.tensor_scalar(top[:, 9:10], top[:, 8:9], -1.0, float(TOPK), ALU.mult, ALU.add))
                step.up(V.tensor_tensor_scan(upto[:, 0:n], equal[:, 0:n], equal[:, 0:n], 0.0, ALU.add, ALU.max))
                step.wait()
                step.up(V.scalar_tensor_tensor(equal[:, 0:n], upto[:, 0:n], top[:, 9:10], equal[:, 0:n],
                                               ALU.is_le, ALU.mult))
                step.wait()
                step.up(V.tensor_tensor(above[:, 0:n], above[:, 0:n], equal[:, 0:n], ALU.add))
                step.wait()
                step.up(V.tensor_scalar(mask[:, tt, 0:n], above[:, 0:n], -1.0, -NEG, ALU.add, ALU.mult))
            for tt in range(NT):
                await_evacuated(dve, T0["b_q"] + tt)
                await_evacuated(dve, T0["b_kv"] + tt)
                rope(qn[:, tt, :], qn[:, tt, :], HEADS, HD // 2, rope2, tt, rope_u, None, rotated["b"])
                rope(bkv[:, tt, 0:P], bkv[:, tt, 0:P], KV_HEADS, HD // 2, rope2, tt, rope_u, None, rotated["b"])

            def attention(base, first_key, mask_of, hi, lo, branch):
                for n, (kind, s) in enumerate(ATTENTION):
                    t = base + n
                    if kind == "logits":
                        tt, h = s // HEADS, s % HEADS
                        nk = tt + 1 - first_key(tt)
                        if s >= 4:
                            await_psum(dve, base + ATTENTION.index(("probs_T", s - 4)))
                        await_psum(dve, t)
                        V.tensor_tensor_reduce(out=probs[:, s % 4, 0:nk * P], in0=ps[:, t % 8, 0:nk * P],
                                               in1=mask_of(tt), scale=-(HD ** -0.5),
                                               scalar=nsink[:, h:h + 1] if branch == 0 else -LOWEST,
                                               op0=ALU.add, op1=ALU.min,
                                               accum_out=nm[:, tt % 2, h:h + 1]).then_inc(evacuated[t % 8], 1)
                    elif kind == "probs_T":
                        tt = s // HEADS
                        nk = tt + 1 - first_key(tt)
                        if s >= 2:
                            await_psum(dve, base + ATTENTION.index(("values", s - 2)))
                        await_psum(dve, t)
                        V.tensor_copy(probs_T[:, s % 2, 0:nk * P], ps[:, t % 8, 0:nk * P]).then_inc(evacuated[t % 8], 1)
                    elif kind == "values":
                        tt, h = s // HEADS, s % HEADS
                        if h < HEADS - 1:
                            continue
                        b = tt % 2
                        if branch == 0:
                            await_evacuated(dve, base + ATTENTION.index(("logits", s)))
                            V.tensor_tensor(sink_e[:, b, :], nm[:, b, :], sink, ALU.add).then_inc(sinks_arg, 1)
                            dve.wait_ge(sinks_exp, tt + 1)
                            step.up(V.tensor_tensor(rs[:, b, :], rs[:, b, :], sink_e[:, b, :], ALU.add))
                            step.wait()
                        dve.wait_ge(probs_made, 32 * branch + s + 1)
                        step.up(V.reciprocal(ri[:, b, :], rs[:, b, :]))
                        for back in range(HEADS):
                            await_evacuated(dve, base + ATTENTION.index(("values", s - back)))
                        step.wait()
                        v3 = o2[:, b, :].rearrange("p (h d) -> p h d", h=HEADS)
                        V.tensor_tensor(v3, v3, ri[:, b, :, None].broadcast_to([P, HEADS, HD]),
                                        ALU.mult).then_inc(o2_made, 1)
                    else:
                        hi_in.take()
                        dst = (slice(None), slice(None), slice(s * P, (s + 1) * P))
                        V.tensor_tensor(lo[dst], bank(t).rearrange("p (k n) -> p k n", k=4),
                                        hi[dst].bitcast(f32), ALU.subtract).then_inc(evacuated[t % 8], 1)

            attention(T0["swa"], lambda tt: max(tt - 1, 0),
                      lambda tt: band[:, 0:2 * P] if tt else band[:, P:2 * P], oTb_hi, oTb_lo, 0)
            for tt in range(NT):
                await_evacuated(dve, T0["a_q"] + tt)
                rope(qn[:, tt, :], qn[:, tt, :], HEADS, HD // 2, rope2, tt, rope_u, None, rotated["a"])
                rope(kn[:, tt, 0:P], kn[:, tt, 0:P], KV_HEADS, HD // 2, rope2, tt, rope_u, None, rotated["a"])
            gate(T0["y_b"], sig_b, T0["g_b"])
            attention(T0["dsa"], lambda tt: 0, lambda tt: mask[:, tt, 0:(tt + 1) * P], oTa_hi, oTa_lo, 1)
            gate_and_merge(T0["y_a"], sig_a, sig_b, sig_a, T0["g_a"], m2_hi, m2_lo, T0["y_b"])
            dve.wait_ge(gains_loaded, 16 * 9)
            boundary("plain", T0["out2"], T0["h4"], slot3, None, 0)
            for half in range(2):
                with dve.Fori(0, 2) as i:
                    for j in range(8):
                        t = T0[f"up2_{half}"] + j
                        await_psum(dve, t, i)
                        if j:
                            dve.wait_ge(f2_made, i * 8 + (16 * half + j))
                        V.tensor_scalar(f2_t[:, j % 4, :], bank(t), 0.0, None, ALU.max).then_inc(evacuated[t % 8], 1)
                        dve.wait_ge(f2_hi_made, i * 8 + (16 * half + j + 1))
                        at_ = bass.ds(i * 8 + j, 1)
                        V.tensor_tensor(f2_lo[:, at_, :], f2_t[:, j % 4:j % 4 + 1, :], f2_hi[:, at_, :].bitcast(f32),
                                        ALU.subtract).then_inc(f2_made, 1)
                if half == 0:
                    for k in range(8):
                        t = T0["down2_0"] + k
                        cc = slice(k % 2 * 512, k % 2 * 512 + 512)
                        await_psum(dve, t)
                        V.tensor_tensor(x[:, k // 2, cc], bank(t), x[:, k // 2, cc],
                                        ALU.add).then_inc(evacuated[t % 8], 1)
            boundary("plain", T0["down2_1"], None, slot4, None, 1)


_INS = {"x": "x", "g_pre_mix": "g_pre_mix", "w_in": "w_in", "ret_decay_logit": "ret_decay_logit",
        "sgu_ln_g": "sgu_ln_g", "sgu_ln_b": "sgu_ln_b", "w_spatial": "w_spatial", "b_spatial": "b_spatial",
        "w_ret_o": "w_ret_o", "w_sgu_o": "w_sgu_o", "w_out": "w_out", "g_post_mix": "g_post_mix",
        "g_pre_ffn": "g_pre_ffn", "w_up": "w_up", "conv_w": "conv_w", "conv_b": "conv_b",
        "w_down": "w_down", "g_post_ffn": "g_post_ffn", "attn_norm": "attn_norm_w_2",
        "w_in2": "w_in_2", "ik_norm_w": "idx_k_norm_w_2", "ik_norm_b": "idx_k_norm_b_2",
        "sinks": "sinks_2", "w_branch_a": "w_branch_a_2", "w_branch_b": "w_branch_b_2",
        "w_out2": "w_out_2", "mlp_norm": "mlp_norm_w_2", "w_up2": "w_up_2", "w_down2": "w_down_2",
        "final_norm": "final_norm_w_2"}
_LAYERED = {"attn_norm", "w_in2", "ik_norm_w", "ik_norm_b", "w_branch_a", "w_branch_b", "w_out2",
            "mlp_norm", "w_up2", "w_down2"}


def _tables(np):
    def rope(half):
        inv = (1.0 / (10000.0 ** (np.arange(half, dtype=np.float64) / half))).astype(np.float32)
        ang = np.arange(S, dtype=np.float32)[:, None] * inv[None, :]
        c, s = np.cos(ang.astype(np.float64)), np.sin(ang.astype(np.float64))
        t = np.stack([c, -s, s], axis=1).astype(np.float32)
        return np.ascontiguousarray(t.reshape(NT, P, 3, half).transpose(1, 0, 2, 3))

    q, k = np.arange(P)[:, None], np.arange(P)[None, :]
    band = np.concatenate([np.where(k > q, 0.0, NEG), np.where(k <= q, 0.0, NEG)], axis=1)
    distance = np.arange(STRIP)[None, :] - (NT - 1) * P - np.arange(P)[:, None]
    return {"rope1": rope(RET_DK // 2), "rope2": rope(HD // 2), "band": band.astype(np.float32),
            "distance": distance.astype(np.float32), "ident": np.eye(P, dtype=np.float32)}


def kernel(**inputs):
    import numpy as _np
    import concourse.bacc as _bacc
    from concourse import mybir as _mybir
    from concourse.bass_utils import run_bass_kernel_spmd as _run

    nc = _bacc.Bacc("TRN2", target_bir_lowering=False, num_devices=1)
    arrays, a = {}, {}

    def declare(name, array):
        arrays[f"in_{name}"] = array
        a[name] = nc.dram_tensor(f"in_{name}", array.shape, _mybir.dt.from_np(array.dtype),
                                 kind="ExternalInput").ap()

    for name, given in _INS.items():
        declare(name, _np.ascontiguousarray(inputs[given]))
        if name in _LAYERED:
            a[name] = a[name][0]
    for name, table in _tables(_np).items():
        declare(name, table)
    out = nc.dram_tensor("out", (1, S, D), _mybir.dt.float32, kind="ExternalOutput").ap()
    two_blocks(nc, a, out)
    r = _run(nc, [arrays], core_ids=[0])
    return r.results[0]["out"]
```

```python
import concourse.bass as bass
from concourse import mybir
from contextlib import ExitStack

P = 128
D = 1024
S = 512
NT = S // P
KT = D // P
RET_H, RET_DK, RET_DV = 4, 128, 256
SGU_G = 4
FF = 2816
FB = FF // P
FF2 = 4096
HD = 64
HEADS, KV_HEADS = 8, 2
TOPK = min(256, S // 4)
EPS = 1e-6
NEG = -1.0e30
LOWEST = -3.0e38
STRIP = (2 * NT - 1) * P

IN1_G = 2 * RET_H * RET_DK + RET_H * RET_DV
IN1_U = IN1_G + RET_H * RET_DV
IN1_SV = IN1_U + D
IN1_AR = IN1_SV + D
IN1_AS = IN1_AR + D
IN2_AK = 512
IN2_IQ2 = 1024
IN2_BQ = 1352
IN2_BK = 1864
IN2_GA = 2120
IN2_GB = 3144
IB_W = IN2_BQ - IN2_IQ2


def attention_events(columns_at):
    events = []
    pairs = NT * HEADS
    for s in range(pairs + 7):
        if s < pairs:
            events.append(("logits", s))
        if 0 <= s - 3 < pairs:
            events.append(("probs_T", s - 3))
        if 0 <= s - 4 < pairs:
            events.append(("values", s - 4))
        done = s - 6
        if done > 0 and done % HEADS == HEADS - 1 and done < pairs:
            events.append(("out_T", done // HEADS))
        if s in columns_at:
            events.append(("column", columns_at.index(s)))
    return events


SWA = attention_events([0, 1, 2, 12, 20, 28, 35, 38])
DSA = attention_events([9, 12, 16, 20, 24, 28, 34, 37])
RETENTION = [("scores", 0), ("scores", 1), ("values", 0), ("scores", 2), ("values", 1),
             ("scores", 3), ("values", 2), ("values", 3)]

TICKETS = [("h1", 8), ("conv_cols", 1), ("spatial_T", 1), ("qkvg", 24), ("qk_T", 8), ("ret", 24), ("sv", 8),
           ("u", 8), ("o_T", 8), ("mix", 8), ("a_ret", 8), ("y_ret", 8), ("a_sgu", 8), ("y_sgu", 8),
           ("out1", 8), ("h2", 8), ("up1", 2 * FB), ("down1", 8), ("h3", 8),
           ("kv_iq", 4), ("iq_ik", 4), ("b_q", 4), ("b_kv", 4), ("i_T", 5), ("index1", 8), ("b_T", 5),
           ("g_b_0", 2), ("index2", 8), ("a_q", 4), ("index3", 8), ("g_b_1", 6), ("a_T", 5),
           ("swa", len(SWA)), ("dsa", len(DSA)), ("y_a", 8),
           ("out2", 8), ("h4", 8),
           ("up2_0", 16), ("down2_0", 8), ("up2_1", 16), ("down2_1", 8)]
UNITS = [("qkvg", 12), ("sv", 4), ("u", 4), ("a_ret", 4), ("y_ret", 4), ("a_sgu", 4), ("y_sgu", 4),
         ("out1", 4), ("up1", FB), ("down1", FB // 2), ("kv_iq", 2), ("iq_ik", 2), ("b_q", 2),
         ("b_kv", 1), ("g_b_0", 1), ("a_q", 2), ("g_b_1", 3), ("g_a", 4), ("y_b", 2), ("y_a", 2), ("out2", 4),
         ("up2_0", 8), ("down2_0", 8), ("up2_1", 8), ("down2_1", 8)]


def starts(parts):
    at, out = 0, {}
    for name, n in parts:
        out[name] = at
        at += n
    return out, at


T0, _ = starts(TICKETS)
U0, N_UNITS = starts(UNITS)
POOL_ADDS = (1, 2)
WARM = 12
UNIT = 2048
GIVEN = [0, *range(U0["up1"] + 2, U0["kv_iq"]), U0["b_q"], *range(U0["up2_0"] + 2, N_UNITS)]


def hi_count(u):
    return sum((v in GIVEN) == (u in GIVEN) for v in range(u + 1))
G_B = [T0["g_b_0"] + n for n in range(2)] + [T0["g_b_1"] + n for n in range(6)]
G_A = [T0["swa"] + SWA.index(("column", n)) for n in range(KT)]
Y_B = [T0["dsa"] + DSA.index(("column", n)) for n in range(KT)]


class Count:

    def __init__(self, engine, sem):
        self.engine, self.sem, self.n = engine, sem, 0

    def up(self, instruction):
        instruction.then_inc(self.sem, 1)
        self.n += 1

    def wait(self):
        if self.n:
            self.engine.wait_ge(self.sem, self.n)

    def take(self, n=1):
        self.n += n
        self.engine.wait_ge(self.sem, self.n)


def two_blocks(nc: bass.Bass, a, out: bass.AP):
    f32 = mybir.dt.float32
    f32r = mybir.dt.float32r
    ALU = mybir.AluOpType
    ACT = mybir.ActivationFunctionType

    ctx = ExitStack()
    with ctx:
        BASE = (nc.sbuf_base + 31) // 32 * 32
        KB = 1024

        def at(name, shape, offset, dt=f32):
            return nc.alloc_sbuf_tensor_at(name, shape, dt, offset=int(BASE + offset))

        x = at("x", [P, NT, D], 0)
        hT_hi = at("hT_hi", [P, KT, S], 16 * KB, f32r)
        hT_lo = at("hT_lo", [P, KT, S], 32 * KB, f32r)
        h_added = at("h_added", [P, KT, S], 16 * KB)
        h_rows = at("h_rows", [P, KT, S], 32 * KB)
        raw = at("raw", [P, 2, UNIT], 48 * KB)
        w_hi = at("w_hi", [P, 2, UNIT], 64 * KB, f32r)
        w_lo = at("w_lo", [P, 2, UNIT], 80 * KB, f32r)
        gain = at("gain", [P, 2, D], 96 * KB)
        mask = at("mask", [P, NT, S], 96 * KB)
        small0 = 104 * KB
        ident = at("ident", [P, P], small0)
        rope2 = at("rope2", [P, NT, 3, HD // 2], small0 + 512)
        band = at("band", [P, 2 * P], small0 + 2048)
        conv = at("conv", [P, 4, 2 * FB], small0 + 3072)
        cells = at("cells", [P, 192], small0 + 3776)
        A = small0 + 3776 + 768
        eps = cells[:, 0:1]
        rms = cells[:, 160:168]
        rstd = cells[:, 168:176]
        sq = cells[:, 4:8]
        sink = cells[:, 8:16]
        nsink = cells[:, 16:24]
        lg = cells[:, 24:32]
        nm = cells[:, 32:48].rearrange("p (t h) -> p t h", t=2)
        rs = cells[:, 48:64].rearrange("p (t h) -> p t h", t=2)
        ri = cells[:, 64:80].rearrange("p (t h) -> p t h", t=2)
        sink_e = cells[:, 80:96].rearrange("p (t h) -> p t h", t=2)
        zero = cells[:, 176:177]
        gm = [cells[:, 96 + 8 * n:104 + 8 * n] for n in range(8)]

        v = at("v", [P, NT, RET_H * RET_DV], A)
        silu_g = at("silu_g", [P, NT, D], A + 16 * KB)
        qk = at("qk", [P, 2, NT, S], A + 32 * KB)
        o = at("o", [P, NT, RET_H, RET_DV], A + 32 * KB)
        qT = at("qT", [P, RET_H, S], A + 48 * KB)
        kT = at("kT", [P, RET_H, S], A + 56 * KB)
        sT = at("sT", [P, 2, NT, S], A + 64 * KB)
        rope_t = at("rope_t", [P, 2, S], A + 64 * KB)
        decay = at("decay", [P, 3, STRIP], A + 80 * KB)
        o_stat = at("o_stat", [P, 104], A + int(92.5 * KB))
        sv_stat = at("sv_stat", [P, 72], A + 87 * KB)
        spatial_T = at("spatial_T", [P, SGU_G, P], A + int(90.5 * KB))
        spatial = at("spatial", [P, SGU_G, P], A)
        conv_rows = at("conv_rows", [2 * FB, 4, P], A + 2 * KB)
        sv = at("sv", [P, NT, D], A + 48 * KB)
        uT = at("uT", [P, KT, S], A + 64 * KB)
        spatial_b = at("spatial_b", [P, SGU_G, P], A + 80 * KB)
        mix_t = at("mix_t", [P, 2, S], A + 82 * KB)
        oT_hi = at("oT_hi", [P, KT, S], A, f32r)
        oT_lo = at("oT_lo", [P, KT, S], A + 16 * KB, f32r)
        yT_hi = at("yT_hi", [P, KT, S], A + 32 * KB, f32r)
        yT_lo = at("yT_lo", [P, KT, S], A + 64 * KB, f32r)
        mT = at("mT", [P, KT, S], A + 48 * KB)
        mT_lo = at("mT_lo", [P, KT, S], A + 48 * KB, f32r)
        mT_hi = at("mT_hi", [P, KT, S], A + 16 * KB, f32r)
        sgu_gate = at("sgu_gate", [P, KT, S], A)
        tables0 = A + 101792 - 4 * (STRIP + NT * 3 * RET_DK // 2)
        distance = at("distance", [P, STRIP], tables0)
        rope1 = at("rope1", [P, NT, 3, RET_DK // 2], tables0 + 4 * STRIP)
        f_hi = at("f_hi", [P, FB, S], A, f32r)
        f_lo = at("f_lo", [P, FB, S], A + 44 * KB, f32r)
        taps = at("taps", [P, 2, 2, S], A + 88 * KB)
        kn = at("kn", [P, NT, S], A)
        ib = at("ib", [P, NT, IB_W], A + 8 * KB)
        qn = at("qn", [P, NT, S], A + int(13.5 * KB))
        oTb = at("oTb", [P, NT, S], A + int(13.5 * KB))
        bkv = at("bkv", [P, NT, 2 * P], A + int(21.5 * KB))
        qT_a = at("qT_a", [P, NT, S], A + int(25.5 * KB))
        ikT = at("ikT", [P, S], A + int(33.5 * KB))
        akT = at("akT", [P, S], A + int(35.5 * KB))
        qT_b = at("qT_b", [P, NT, S], A + int(37.5 * KB))
        bkT = at("bkT", [P, S], A + int(45.5 * KB))
        score = at("score", [P, S], A + int(47.5 * KB))
        work = at("work", [P, S], A + int(49.5 * KB))
        relu = at("relu", [P, HEADS, S], A + int(81.5 * KB))
        rope_u = at("rope_u", [P, 2, S], A + int(55.5 * KB))
        probs = at("probs", [P, 4, S], A + int(47.5 * KB))
        probs_T = at("probs_T", [P, 2, S], A + int(55.5 * KB))
        o2 = at("o2", [P, 2, S], A + int(59.5 * KB))
        above = at("above", [P, S], A + int(55.5 * KB))
        equal = at("equal", [P, S], A + int(57.5 * KB))
        upto = at("upto", [P, S], A + int(59.5 * KB))
        ik2 = at("ik2", [P, NT, 2, HD], A + int(61.5 * KB))
        ik_gain = at("ik_gain", [P, 2, HD], A + int(63.5 * KB))
        ik_stat = at("ik_stat", [P, 64], A + 64 * KB)
        top = at("top", [P, 16], A + int(64.5 * KB))
        sig_b = at("sig_b", [P, KT, S], A + int(65.5 * KB))
        sig_a = at("sig_a", [P, KT, S], A + int(81.5 * KB))
        m2_lo = at("m2_lo", [P, KT, S], A + int(81.5 * KB), f32r)
        m2_hi = at("m2_hi", [P, KT, S], A, f32r)
        oTb_hi = at("oTb_hi", [P, NT, S], 16 * KB, f32r)
        oTb_lo = at("oTb_lo", [P, NT, S], 24 * KB, f32r)
        oTa_hi = at("oTa_hi", [P, NT, S], 32 * KB, f32r)
        oTa_lo = at("oTa_lo", [P, NT, S], 40 * KB, f32r)
        f2_hi = at("f2_hi", [P, 16, S], A, f32r)
        f2_lo = at("f2_lo", [P, 16, S], A + 32 * KB, f32r)
        f2_t = at("f2_t", [P, 4, S], A + 64 * KB)
        out_rows = at("out_rows", [P, NT, D], A + 72 * KB)

        ps = ctx.enter_context(nc.psum_tensor("ps", [P, 8, S], f32))

        def sem(name):
            return ctx.enter_context(nc.semaphore(name))

        x_loaded = [sem(f"x_loaded{t}") for t in range(NT)]
        tables_loaded = sem("tables_loaded")
        gains_loaded = sem("gains_loaded")
        raw_loaded = [sem(f"raw_loaded{s}") for s in range(2)]
        unit_hi = sem("unit_hi")
        hi_given = sem("hi_given")
        unit_split = sem("unit_split")
        first_low = sem("first_low")
        unit_started = sem("unit_started")
        psum_ready = sem("psum_ready")
        evacuated = [sem(f"evacuated{b}") for b in range(8)]
        dve_step = sem("dve_step")
        act_step = sem("act_step")
        eps_set = sem("eps_set")
        zero_set = sem("zero_set")
        rms_made = sem("rms_made")
        x_updated = sem("x_updated")
        x_added = sem("x_added")
        h_made = sem("h_made")
        hi_made = sem("hi_made")
        spatial_b_loaded = sem("spatial_b_loaded")
        ik_gain_loaded = sem("ik_gain_loaded")
        ident_loaded = sem("ident_loaded")
        hot = sem("hot")
        lo_made = sem("lo_made")
        gamma_arg = sem("gamma_arg")
        gamma_exp = sem("gamma_exp")
        decay_arg = sem("decay_arg")
        decay_made = sem("decay_made")
        qk_rotated = sem("qk_rotated")
        o_stats = sem("o_stats")
        o_rms = sem("o_rms")
        o_gated = sem("o_gated")
        sv_stats = sem("sv_stats")
        sv_rms = sem("sv_rms")
        sv_normed = sem("sv_normed")
        centre = sem("centre")
        left = sem("left")
        gelu_made = sem("gelu_made")
        gated = sem("gated")
        f_hi_made = sem("f_hi_made")
        f_made = sem("f_made")
        ik_stats = sem("ik_stats")
        ik_rms = sem("ik_rms")
        i_rotated = sem("i_rotated")
        b_rotated = sem("b_rotated")
        a_rotated = sem("a_rotated")
        probs_made = sem("probs_made")
        sigmoids_made = sem("sigmoids_made")
        sinks_arg = sem("sinks_arg")
        sinks_exp = sem("sinks_exp")
        o2_made = sem("o2_made")
        squared = sem("squared")
        f2_hi_made = sem("f2_hi_made")
        f2_made = sem("f2_made")
        out_made = sem("out_made")
        stored = sem("stored")

        def bank(t):
            return ps[:, t % 8, :]

        def await_psum(engine, t, i=0):
            engine.wait_ge(psum_ready, i * 8 + (t + 1))

        def await_evacuated(engine, t, i=0):
            engine.wait_ge(evacuated[t % 8], i + (t // 8 + 1))

        block = ctx.enter_context(nc.Block())

        @block.sync
        def _(sp):
            def load(u, src, k, i=0, per=0):
                if u >= 2 or per:
                    sp.wait_ge(unit_split, i * (2 * per) + 2 * (u - 1))
                if len(src.shape) == 4:
                    dst = raw[:, u % 2, :].rearrange("p (k h n) -> p k h n", k=k, h=2)
                    parts = [(dst[:, :, h, :], src[:, :, h, :]) for h in range(2)]
                else:
                    dst = raw[:, u % 2, 0:k * src.shape[2]].rearrange("p (k n) -> p k n", k=k)
                    parts = [(dst[:, h:h + k // 2, :], src[:, h:h + k // 2, :]) for h in (0, k // 2)]
                for part, of in parts:
                    sp.dma_start(part, of).then_inc(raw_loaded[u % 2], 16)

            def load_x(t):
                sp.dma_start(x[:, t, :], a["x"][0, t * P:(t + 1) * P, :]).then_inc(x_loaded[t], 16)

            load_x(0)
            sp.dma_start(gain[:, 0, :], a["g_pre_mix"].partition_broadcast(P)).then_inc(gains_loaded, 16)
            load_x(1)
            sp.dma_start(ident[:, :], a["ident"]).then_inc(ident_loaded, 16)

            def rows(name):
                return a[name].rearrange("(k p) n -> p k n", p=P)

            def wide(name, c, n=512):
                w = rows(name)
                return [w[:, h * 4:h * 4 + 4, c:c + n] for h in range(2)]

            w1 = rows("w_in")
            u = U0["qkvg"]
            for h, src in enumerate(wide("w_in", 0)):
                load(u + h, src, 4)
                for t in ((2,), (3,))[h]:
                    load_x(t)
            for src, dst in ((a["rope1"], rope1), (a["distance"], distance), (a["rope2"], rope2), (a["band"], band)):
                sp.dma_start(dst[:], src).then_inc(tables_loaded, 16)
            sp.dma_start(lg, a["ret_decay_logit"].rearrange("a h -> (a h)").partition_broadcast(P)).then_inc(
                tables_loaded, 16)
            sp.dma_start(sink, a["sinks"][0, :].partition_broadcast(P)).then_inc(tables_loaded, 16)
            sp.dma_start(spatial[:, :, :], a["w_spatial"].rearrange("g p q -> p g q")).then_inc(tables_loaded, 16)
            sp.dma_start(conv_rows[:, 0:3, :], a["conv_w"].rearrange("t (j c) -> j t c", c=P)).then_inc(
                tables_loaded, 16)
            sp.dma_start(conv_rows[:, 3, :], a["conv_b"].rearrange("(j c) -> j c", c=P)).then_inc(tables_loaded, 16)
            for h, src in enumerate(wide("w_in", 512)):
                load(u + 2 + h, src, 4)
            with sp.Fori(1, 3) as i:
                for b in range(2):
                    for h in range(2):
                        load(u + 2 * b + h, w1[:, h * 4:h * 4 + 4, bass.ds(i * 1024 + b * 512, 512)], 4, i, 4)
            for b in range(2):
                for h, src in enumerate(wide("w_in", IN1_SV + b * 512)):
                    load(U0["sv"] + 2 * b + h, src, 4)

            def narrow(phase, name, c, n=4):
                for j in range(n):
                    load(U0[phase] + j, rows(name)[:, :, c + j * 256:c + j * 256 + 256], KT)

            narrow("u", "w_in", IN1_U)
            narrow("a_ret", "w_in", IN1_AR)
            narrow("y_ret", "w_ret_o", 0)
            narrow("a_sgu", "w_in", IN1_AS)
            narrow("y_sgu", "w_sgu_o", 0)

            def long(phase, name, n, row0=0):
                w = rows(name)
                with sp.Fori(0, n // 2) as i:
                    for j in range(2):
                        load(U0[phase] + j, w[:, bass.ds(i * 4 + (row0 + 2 * j), 2), :], 2, i, 2)
                if n % 2:
                    load(U0[phase] + n - 1, w[:, row0 + 2 * n - 2:row0 + 2 * n, :], 2)

            long("out1", "w_out", 4)
            up = a["w_up"].rearrange("(k p) (h j n) -> p k h j n", p=P, h=2, n=P)
            with sp.Fori(0, FB // 2) as i:
                for j in range(2):
                    blocks = up[:, :, :, bass.ds(i * 2 + j, 1), :].rearrange("p k h a n -> p k h (a n)")
                    load(U0["up1"] + j, blocks, KT, i, 2)
            long("down1", "w_down", FB // 2)

            def load_wide2(phase, c, n=512):
                for h, src in enumerate(wide("w_in2", c, n)):
                    load(U0[phase] + h, src, 4)

            load_wide2("kv_iq", IN2_AK)
            load_wide2("iq_ik", IN2_IQ2, IB_W)
            load_wide2("b_q", IN2_BQ)
            load(U0["b_kv"], rows("w_in2")[:, :, IN2_BK:IN2_GA], KT)
            narrow("g_b_0", "w_in2", IN2_GB, 1)
            load_wide2("a_q", 0)
            narrow("g_b_1", "w_in2", IN2_GB + 256, 3)
            narrow("g_a", "w_in2", IN2_GA)
            for phase, name in (("y_b", "w_branch_b"), ("y_a", "w_branch_a")):
                for j in range(2):
                    load(U0[phase] + j, rows(name)[:, :, j * 512:j * 512 + 512], 4)
            long("out2", "w_out2", 4)
            w_up2 = rows("w_up2")
            for half in range(2):
                with sp.Fori(0, 4) as i:
                    for j in range(2):
                        load(U0[f"up2_{half}"] + j,
                             w_up2[:, :, bass.ds(i * 512 + (half * 2048 + j * 256), 256)], KT, i, 2)
                long(f"down2_{half}", "w_down2", 8, 16 * half)
            for t in range(NT):
                sp.wait_ge(out_made, t + 1)
                sp.dma_start(out[0, t * P:(t + 1) * P, :], out_rows[:, t, :]).then_inc(stored, 16)
            sp.wait_ge(stored, 16 * NT)

        @block.gpsimd
        def _(pool):
            x_out = Count(pool, x_updated)

            def split(u, i=0, last=None, first=False, n=UNIT):
                s = u % 2
                given = u in GIVEN
                if not given:
                    pool.wait_ge(raw_loaded[s], i * 32 + 32 * (u // 2 + 1))
                    if last is not None:
                        await_psum(pool, last)
                    elif u >= 2:
                        pool.wait_ge(unit_started, i * 2 + u)
                    nc.gpsimd.tensor_tensor(w_hi[:, s, 0:n], raw[:, s, 0:n], zero.broadcast_to([P, n]),
                                            ALU.add).then_inc(unit_hi, 1)
                pool.wait_ge(hi_given if given else unit_hi, i * 2 + hi_count(u))
                for half in range(2):
                    c = slice(half * n // 2, (half + 1) * n // 2)
                    if first:
                        c = slice((2 + half) * n // 4, (3 + half) * n // 4)
                    if first and half == 1:
                        pool.wait_ge(first_low, 1)
                    nc.gpsimd.tensor_tensor(w_lo[:, s, c], raw[:, s, c], w_hi[:, s, c].bitcast(f32),
                                            ALU.subtract).then_inc(unit_split, 1)

            def split_all(u, end):
                if u % 2:
                    split(u)
                    u += 1
                with pool.Fori(0, (end - u) // 2) as i:
                    for s in range(2):
                        split(u + s, i)
                if (end - u) % 2:
                    split(end - 1)

            def boundary(tin):
                for tt in POOL_ADDS:
                    for half in range(2):
                        await_evacuated(pool, tin + 2 * tt + half)
                    row = x[:, tt, :].rearrange("p (k n) -> p k n", k=KT)
                    x_out.up(nc.gpsimd.tensor_tensor(row, row, h_added[:, :, tt * P:(tt + 1) * P], ALU.add))

            nc.gpsimd.memset(zero, 0.0).then_inc(zero_set, 1)
            pool.wait_ge(zero_set, 1)
            split(0, first=True)
            split(1)
            split_all(2, U0["up1"] + 1)
            boundary(T0["out1"])
            split(U0["up1"] + 1, last=T0["h2"] - 1)
            split_all(U0["up1"] + 2, U0["kv_iq"])
            split(U0["kv_iq"])
            boundary(T0["down1"])
            split(U0["kv_iq"] + 1, last=T0["h3"] - 1)
            for h in range(2):
                split(U0["iq_ik"] + h, n=4 * IB_W)
            split(U0["b_q"])
            split_all(U0["b_q"] + 1, U0["up2_0"] + 2)
            split_all(U0["up2_0"] + 2, N_UNITS)

        @block.tensor
        def _(pe):
            h_in = Count(pe, h_made)

            def claim(t, i=0):
                if t >= 8:
                    pe.wait_ge(evacuated[t % 8], i + t // 8)

            def three(dst, a_hi, a_lo, b_hi, b_lo, start, stop):
                first = nc.tensor.matmul(dst, a_hi, b_hi, start=start, stop=False)
                nc.tensor.matmul(dst, a_hi, b_lo, start=False, stop=False)
                return first, nc.tensor.matmul(dst, a_lo, b_hi, start=False, stop=stop)

            def weights(u, k, n, i=0, per=0, wait=True):
                if wait:
                    pe.wait_ge(unit_split, i * (2 * per) + 2 * (u + 1))
                return [w[:, u % 2, 0:k * n].rearrange("p (k n) -> p k n", k=k) for w in (w_hi, w_lo)]

            def first_T(u, t, phase):
                for tt in range(2):
                    h_transposes(phase, tt)
                    keep_warm(T0[phase] + 2 * tt + 2, WARM)
                hi, lo = weights(u, KT, 256)
                for half in range(2):
                    for tt in (2 * half, 2 * half + 1):
                        await_h(phase, tt)
                    tok = slice(half * S // 2, (half + 1) * S // 2)
                    for c in range(2):
                        if half == 0:
                            if c == 1:
                                for tt in (2, 3):
                                    h_transposes(phase, tt)
                            claim(t + c)
                        cc = slice(c * P, (c + 1) * P)
                        for kk in range(KT):
                            first, last = three(ps[:, (t + c) % 8, tok], hi[:, kk, cc], lo[:, kk, cc],
                                                hT_hi[:, kk, tok], hT_lo[:, kk, tok], kk == 0, kk == KT - 1)
                            if half == 0 and c == 0 and kk == 0:
                                first.then_inc(unit_started, 1)
                        if half == 1:
                            last.then_inc(psum_ready, 1)

            def column(u, t, k, n, c, r_hi, r_lo, i=0, per=0, ready=None):
                hi, lo = weights(u, k, n, i, per, wait=c == 0)
                claim(t, i)
                for kk in range(k):
                    if ready:
                        ready(kk)
                    cc = slice(c * P, (c + 1) * P)
                    first, last = three(bank(t), hi[:, kk, cc], lo[:, kk, cc], r_hi[:, kk, :],
                                        r_lo[:, kk, :], kk == 0, kk == k - 1)
                    if c == 0 and kk == 0:
                        first.then_inc(unit_started, 1)
                last.then_inc(psum_ready, 1)

            def unit_T(u, t, k, n, r_hi, r_lo, i=0, per=0, ready=None):
                for c in range(n // P):
                    column(u, t + c, k, n, c, r_hi, r_lo, i, per, None if c else ready)

            def unit_N(u, t, k, n, k0, start, stop, i=0, per=0, after=None):
                for tt in range(NT):
                    if after:
                        for next_ in ((0, 1), (2,), (3,), ())[tt]:
                            h_transposes(after, next_)
                            if after == "h1" and next_ == NT - 1:
                                table_transposes()
                            if next_ == (1 if after == "h1" else 0):
                                keep_warm(T0[after] + 2 * next_ + 2, WARM)
                        await_h(after, tt)
                    if tt == 0:
                        hi, lo = weights(u, k, n, i, per)
                    if start:
                        claim(t + tt, i)
                    tok = slice(tt * P, (tt + 1) * P)
                    for kk in range(k):
                        first, last = three(ps[:, (t + tt) % 8, 0:n], hT_hi[:, k0 + kk, tok],
                                            hT_lo[:, k0 + kk, tok], hi[:, kk, :], lo[:, kk, :],
                                            start and kk == 0, stop and kk == k - 1)
                        if tt == 0 and kk == 0:
                            first.then_inc(unit_started, 1)
                    if stop:
                        last.then_inc(psum_ready, 1)

            def unit_L(u, t, k0, l_hi, l_lo, start, stop, ready):
                hi, lo = weights(u, 2, D)
                for kk in range(2):
                    ready(k0 + kk)
                for tt in range(NT):
                    tok = slice(tt * P, (tt + 1) * P)
                    for half in range(2):
                        if start:
                            claim(t + 2 * tt + half)
                        for kk in range(2):
                            cc = slice(half * 512, half * 512 + 512)
                            first, last = three(bank(t + 2 * tt + half), l_hi[:, k0 + kk, tok],
                                                l_lo[:, k0 + kk, tok], hi[:, kk, cc], lo[:, kk, cc],
                                                start and kk == 0, stop and kk == 1)
                            if tt == 0 and half == 0 and kk == 0:
                                first.then_inc(unit_started, 1)
                        if stop:
                            last.then_inc(psum_ready, 1)

            def long(phase, n, l_hi, l_lo, ready):
                for j in range(n):
                    unit_L(U0[phase] + j, T0[phase], 2 * j, l_hi, l_lo, j == 0, j == n - 1, ready)

            def transposes(t, blocks, width=P):
                claim(t)
                for n, src in enumerate(blocks):
                    k = src.shape[0]
                    last = nc.tensor.transpose(ps[:, t % 8, n * width:n * width + width], src, ident[0:k, 0:k])
                last.then_inc(psum_ready, 1)

            def h_transposes(phase, tt):
                h_in.take()
                for half in range(2):
                    transposes(T0[phase] + 2 * tt + half,
                               [h_rows[:, 4 * half + n, tt * P:(tt + 1) * P] for n in range(4)])

            def keep_warm(t, n):
                claim(t)
                for _ in range(n):
                    nc.tensor.transpose(bank(t)[:, 0:P], ident[:, :], ident[:, :])

            def await_h(phase, tt):
                for half in range(2):
                    await_evacuated(pe, T0[phase] + 2 * tt + half)

            def narrow(phase, r_hi, r_lo, ready=None):
                for j in range(4):
                    unit_T(U0[phase] + j, T0[phase] + 2 * j, KT, 256, r_hi, r_lo, ready=ready if j == 0 else None)

            def wide(phase, n=512, after=None):
                for h in range(2):
                    unit_N(U0[phase] + h, T0[phase], 4, n, 4 * h, h == 0, h == 1, after=None if h else after)

            def table_transposes():
                pe.wait_ge(tables_loaded, 16 * 9)
                transposes(T0["conv_cols"], [conv_rows[:, n, :] for n in range(4)], 2 * FB)
                transposes(T0["spatial_T"], [spatial[:, g, :] for g in range(SGU_G)])

            pe.wait_ge(ident_loaded, 16)
            for b in range(2):
                for h in range(2):
                    unit_N(U0["qkvg"] + 2 * b + h, T0["qkvg"] + 4 * b, 4, 512, 4 * h, h == 0, h == 1,
                           after=None if b or h else "h1")
            with pe.Fori(1, 3) as i:
                for b in range(2):
                    for h in range(2):
                        unit_N(U0["qkvg"] + 2 * b + h, T0["qkvg"] + 4 * b, 4, 512, 4 * h, h == 0, h == 1, i, 4)
            for tt in range(NT):
                for w in range(2):
                    pe.wait_ge(qk_rotated, 4 * w + tt + 1)
                    transposes(T0["qk_T"] + 2 * tt + w, [qk[:, w, tt, h * P:(h + 1) * P] for h in range(RET_H)])
            for t in range(T0["qk_T"], T0["qk_T"] + 8):
                await_evacuated(pe, t)
            t = T0["ret"]
            held = {}
            for kind, h in RETENTION:
                if kind == "scores":
                    for mb in range(NT):
                        claim(t)
                        nc.tensor.matmul(bank(t), kT[:, h, mb * P:(mb + 1) * P], qT[:, h, :],
                                         start=True, stop=True).then_inc(psum_ready, 1)
                        held[h, mb] = t
                        t += 1
                else:
                    for mb in range(NT):
                        await_evacuated(pe, held[h, mb])
                    for pair in range(2):
                        claim(t)
                        for nn in range(2):
                            n0 = (2 * pair + nn) * P
                            for mb in range(NT):
                                last = nc.tensor.matmul(ps[:, t % 8, nn * 256:nn * 256 + 256],
                                                        sT[:, h % 2, mb, n0:n0 + P],
                                                        v[:, mb, h * RET_DV:(h + 1) * RET_DV],
                                                        start=mb == 0, stop=mb == NT - 1)
                        last.then_inc(psum_ready, 1)
                        t += 1
            for b in range(2):
                for h in range(2):
                    unit_N(U0["sv"] + 2 * b + h, T0["sv"] + 4 * b, 4, 512, 4 * h, h == 0, h == 1)
            narrow("u", hT_hi, hT_lo)
            for tt in range(NT):
                pe.wait_ge(o_gated, tt + 1)
                for half in range(2):
                    transposes(T0["o_T"] + 2 * tt + half,
                               [o[:, tt, 2 * half + n // 2, n % 2 * P:n % 2 * P + P] for n in range(4)])
            pe.wait_ge(sv_normed, NT)
            for c in range(KT):
                t = T0["mix"] + c
                claim(t)
                for n in range(NT):
                    last = nc.tensor.matmul(ps[:, t % 8, n * P:(n + 1) * P], sv[:, n, c * P:(c + 1) * P],
                                            spatial_T[:, c // 2, :], start=True, stop=True)
                last.then_inc(psum_ready, 1)
            narrow("a_ret", hT_hi, hT_lo)
            for tt in range(NT):
                await_h("o_T", tt)
            narrow("y_ret", oT_hi, oT_lo)
            narrow("a_sgu", hT_hi, hT_lo)
            narrow("y_sgu", yT_hi, yT_lo, ready=lambda k: pe.wait_ge(lo_made, k + 1))
            long("out1", 4, mT_hi, mT_lo, ready=lambda k: pe.wait_ge(lo_made, KT + k + 1))
            t, u = T0["up1"], U0["up1"]
            first_T(u, t, "h2")
            for j in range(1, 4):
                unit_T(u + j, t + 2 * j, KT, 256, hT_hi, hT_lo)
            with pe.Fori(1, FB // 4) as i:
                for j in range(4):
                    unit_T(u + j, t + 2 * j, KT, 256, hT_hi, hT_lo, i, 4)
            for j in range(FB // 4 * 4, FB):
                unit_T(u + j, t + 2 * j, KT, 256, hT_hi, hT_lo)
            long("down1", FB // 2, f_hi, f_lo, ready=lambda k: pe.wait_ge(f_made, k + 1))

            def head_pairs(src, tt, t):
                transposes(t, [src[:, tt, r * P:(r + 1) * P] for r in range(4)])

            def await_tickets(base, n):
                for t in range(base, base + n):
                    await_evacuated(pe, t)

            def index_scores(tt):
                n = (tt + 1) * P
                for h in range(HEADS):
                    t = T0[f"index{tt}"] + h
                    claim(t)
                    r = slice(HD * (h % 2), HD * (h % 2) + HD)
                    nc.tensor.matmul(ps[:, t % 8, 0:n], qT_a[r, h // 2, tt * P:(tt + 1) * P], ikT[r, 0:n],
                                     start=True, stop=True).then_inc(psum_ready, 1)

            wide("kv_iq", after="h3")
            wide("iq_ik", IB_W)
            wide("b_q")
            unit_N(U0["b_kv"], T0["b_kv"], KT, 256, 0, True, True)
            for tt in range(NT):
                pe.wait_ge(i_rotated, 3 * tt + 3)
                transposes(T0["i_T"] + tt, [kn[:, tt, 256:384], kn[:, tt, 384:512], ib[:, tt, 0:P], ib[:, tt, P:2 * P]])
            transposes(T0["i_T"] + 4, [ik2[:, tt, :, :].rearrange("p a d -> p (a d)") for tt in range(NT)])
            await_tickets(T0["i_T"], 5)
            index_scores(1)
            for tt in range(NT):
                pe.wait_ge(b_rotated, 2 * tt + 2)
                head_pairs(qn, tt, T0["b_T"] + tt)
            transposes(T0["b_T"] + 4, [bkv[:, tt, 0:P] for tt in range(NT)])
            unit_T(U0["g_b_0"], T0["g_b_0"], KT, 256, hT_hi, hT_lo)
            index_scores(2)
            wide("a_q")
            index_scores(3)
            for j in range(3):
                unit_T(U0["g_b_1"] + j, T0["g_b_1"] + 2 * j, KT, 256, hT_hi, hT_lo)
            for tt in range(NT):
                pe.wait_ge(a_rotated, 2 * tt + 2)
                head_pairs(qn, tt, T0["a_T"] + tt)
            transposes(T0["a_T"] + 4, [kn[:, tt, 0:P] for tt in range(NT)])

            def ga_column(c):
                column(U0["g_a"] + c // 2, G_A[c], KT, 256, c % 2, hT_hi, hT_lo)

            def yb_column(c):
                if c == 0:
                    pe.wait_ge(lo_made, 2 * KT + NT)
                column(U0["y_b"] + c // 4, Y_B[c], 4, 512, c % 4, oTb_hi, oTb_lo)

            def attention(events, base, q, k, val, first_key, outs, other):
                t = base
                held = {}
                for kind, s in events:
                    if kind == "column":
                        other(s)
                        t += 1
                        continue
                    tt, h = (s // HEADS, s % HEADS) if kind != "out_T" else (s, 0)
                    r = slice(HD * (h // 4), HD * (h // 4) + HD)
                    k0 = first_key(tt)
                    nk = tt + 1 - k0
                    claim(t)
                    held[kind, s] = t
                    if kind == "logits":
                        nc.tensor.matmul(ps[:, t % 8, 0:nk * P], q[r, h % 4, tt * P:(tt + 1) * P],
                                         k[r, k0 * P:(tt + 1) * P], start=True, stop=True).then_inc(psum_ready, 1)
                    elif kind == "probs_T":
                        pe.wait_ge(probs_made, outs * 32 + s + 1)
                        for n in range(nk):
                            last = nc.tensor.transpose(ps[:, t % 8, n * P:(n + 1) * P],
                                                       probs[:, s % 4, n * P:(n + 1) * P], ident[:, :])
                        last.then_inc(psum_ready, 1)
                    elif kind == "values":
                        await_evacuated(pe, held["probs_T", s])
                        for n in range(nk):
                            last = nc.tensor.matmul(ps[:, t % 8, 0:HD], probs_T[:, s % 2, n * P:(n + 1) * P],
                                                    val(k0 + n, h // 4), start=n == 0, stop=n == nk - 1)
                        last.then_inc(psum_ready, 1)
                    else:
                        pe.wait_ge(o2_made, outs * NT + tt + 1)
                        for n in range(4):
                            last = nc.tensor.transpose(ps[:, t % 8, n * P:(n + 1) * P],
                                                       o2[:, tt % 2, n * P:(n + 1) * P], ident[:, :])
                        last.then_inc(psum_ready, 1)
                    t += 1
                return [held["out_T", tt] for tt in range(NT)]

            await_tickets(T0["b_T"], 5)
            attention(SWA, T0["swa"], qT_b, bkT, lambda kb, g: bkv[:, kb, P + g * HD:P + (g + 1) * HD],
                      lambda tt: max(tt - 1, 0), 0, ga_column)
            await_tickets(T0["a_T"], 5)
            for t in attention(DSA, T0["dsa"], qT_a, akT, lambda kb, g: kn[:, kb, P + g * HD:P + (g + 1) * HD],
                               lambda tt: 0, 1, yb_column):
                await_evacuated(pe, t)
            for j in range(2):
                unit_T(U0["y_a"] + j, T0["y_a"] + 4 * j, 4, 512, oTa_hi, oTa_lo)
            long("out2", 4, m2_hi, m2_lo, ready=lambda k: pe.wait_ge(lo_made, 2 * KT + NT + k + 1))
            for half in range(2):
                t, u = T0[f"up2_{half}"], U0[f"up2_{half}"]
                for j in range(8):
                    if half == 0 and j == 0:
                        first_T(u, t, "h4")
                    else:
                        unit_T(u + j, t + 2 * j, KT, 256, hT_hi, hT_lo)
                long(f"down2_{half}", 8, f2_hi, f2_lo,
                     ready=lambda k, half=half: pe.wait_ge(f2_made, 16 * half + k + 1))

        STEPS = [("A", 0), ("A", 1), ("B", 0), ("A", 2), ("B", 1), ("C", 0), ("C", 1), ("A", 3),
                 ("B", 2), ("B", 3), ("C", 2), ("C", 3)]

        @block.scalar
        def _(act):
            step = Count(act, act_step)
            rms_out = Count(act, rms_made)
            x_in = Count(act, x_updated)
            x_added_in = Count(act, x_added)
            hi_out = Count(act, hi_made)
            hot_in = Count(act, hot)

            def evacuate(t, dst, func, src=None):
                await_psum(act, t)
                nc.scalar.activation(dst, bank(t) if src is None else src, func).then_inc(evacuated[t % 8], 1)

            def give_hi(u, i=0, per=0, started=False):
                s = u % 2
                act.wait_ge(raw_loaded[s], i * (16 * per) + 32 * (u // 2 + 1))
                if started:
                    act.wait_ge(unit_started, u)
                nc.scalar.activation(w_hi[:, s, :], raw[:, s, :], ACT.Copy).then_inc(hi_given, 1)

            def load_gain(n, src):
                act.dma_start(gain[:, n, :], src.partition_broadcast(P)).then_inc(gains_loaded, 16)

            def boundary(kind, tin, tout):
                step.up(nc.scalar.activation(sq[:, 1:2], eps, ACT.Sqrt))
                for which, tt in STEPS:
                    tok = slice(tt * P, (tt + 1) * P)
                    rms_out.wait()
                    if which == "A" and kind == "norm":
                        b = (tin + 2 * tt) % 8
                        await_psum(act, tin + 2 * tt + 1)
                        step.up(nc.scalar.activation(h_added[:, :, tok],
                                                     ps[:, b:b + 2, :].rearrange("p b (k n) -> p (b k) n", k=4),
                                                     ACT.Square, accum_out=sq[:, 0:1]))
                        step.wait()
                        rms_out.up(nc.scalar.activation(rms[:, 2 * tt:2 * tt + 1], sq[:, 0:1], ACT.Sqrt,
                                                        bias=eps, scale=1.0 / D))
                    elif which == "B":
                        if kind == "none":
                            act.wait_ge(x_loaded[tt], 16)
                        elif kind == "plain":
                            for half in range(2):
                                await_evacuated(act, tin + 2 * tt + half)
                        else:
                            (x_in if tt in POOL_ADDS else x_added_in).take()
                        squares = out_rows[:, tt, :] if tout is None else h_rows[:, :, tok]
                        row = x[:, tt, :] if tout is None else x[:, tt, :].rearrange("p (k n) -> p k n", k=KT)
                        step.up(nc.scalar.activation(squares, row, ACT.Square, accum_out=sq[:, 3:4]))
                        step.wait()
                        rms_out.up(nc.scalar.activation(rms[:, 2 * tt + 1:2 * tt + 2], sq[:, 3:4], ACT.Sqrt,
                                                        bias=eps, scale=1.0 / D))
                        if kind == "none" and tt == 1:
                            give_hi(0)
                    elif which == "C" and tout is not None:
                        for half in range(2):
                            t = tout + 2 * tt + half
                            await_psum(act, t)
                            hi_out.up(nc.scalar.activation(
                                hT_hi[:, 4 * half:4 * half + 4, tt * P:(tt + 1) * P],
                                bank(t).rearrange("p (k n) -> p k n", k=4), ACT.Copy))

            act.wait_ge(eps_set, 1)
            boundary("none", None, T0["h1"])
            evacuate(T0["conv_cols"], conv[:, :, :], ACT.Copy,
                     ps[:, T0["conv_cols"] % 8, 0:8 * FB].rearrange("p (t j) -> p t j", t=4))
            evacuate(T0["spatial_T"], spatial_T[:, :, :], ACT.Copy,
                     bank(T0["spatial_T"]).rearrange("p (g q) -> p g q", g=SGU_G))
            act.wait_ge(gamma_arg, 1)
            nc.scalar.activation(gm[2], gm[1], ACT.Exp).then_inc(gamma_exp, 1)

            def decay_exp(h):
                act.wait_ge(decay_arg, h + 1)
                nc.scalar.activation(decay[:, h % 2, :], decay[:, h % 2, :], ACT.Exp).then_inc(decay_made, 1)

            decay_exp(0)
            decay_exp(1)
            await_evacuated(act, T0["h1"] + 7)
            load_gain(0, a["sgu_ln_g"])
            load_gain(1, a["sgu_ln_b"])
            for b in range(2):
                for tt in range(NT):
                    evacuate(T0["qkvg"] + 8 + 4 * b + tt, v[:, tt, b * 512:b * 512 + 512], ACT.Copy)
            for b in range(2):
                for tt in range(NT):
                    evacuate(T0["qkvg"] + 16 + 4 * b + tt, silu_g[:, tt, b * 512:b * 512 + 512], ACT.Silu)
            for tt in range(NT):
                for w, dst in ((0, qT), (1, kT)):
                    t = T0["qk_T"] + 2 * tt + w
                    evacuate(t, dst[:, :, tt * P:(tt + 1) * P], ACT.Copy,
                             bank(t).rearrange("p (h n) -> p h n", h=RET_H))
            t = T0["ret"]
            for kind, h in RETENTION:
                if kind == "scores":
                    t += NT
                    continue
                if h + 2 < RET_H:
                    decay_exp(h + 2)
                for pair in range(2):
                    evacuate(t, o[:, 2 * pair:2 * pair + 2, h, :], ACT.Copy,
                             bank(t).rearrange("p (n e) -> p n e", n=2))
                    t += 1
            act.wait_ge(o_stats, NT * RET_H)
            nc.scalar.activation(o_stat[:, 60:76], o_stat[:, 13:45:2], ACT.Sqrt, bias=eps).then_inc(o_rms, 1)
            for b in range(2):
                for tt in range(NT):
                    evacuate(T0["sv"] + 4 * b + tt, sv[:, tt, b * 512:b * 512 + 512], ACT.Gelu_apprx_tanh)
            await_evacuated(act, T0["ret"] + 19)
            act.dma_start(spatial_b[:, :, :].rearrange("p g q -> p (g q)"),
                          a["b_spatial"].rearrange("g q -> (g q)").partition_broadcast(P)).then_inc(
                              spatial_b_loaded, 16)
            act.wait_ge(sv_stats, NT)
            nc.scalar.activation(sv_stat[:, 64:68], sv_stat[:, 49:57:2], ACT.Sqrt, bias=eps).then_inc(sv_rms, 1)
            for c in range(KT):
                evacuate(T0["u"] + c, uT[:, c, :], ACT.Gelu_apprx_tanh)
            for tt in range(NT):
                for half in range(2):
                    t = T0["o_T"] + 2 * tt + half
                    await_psum(act, t)
                    hi_out.up(nc.scalar.activation(oT_hi[:, 4 * half:4 * half + 4, tt * P:(tt + 1) * P],
                                                   bank(t).rearrange("p (k n) -> p k n", k=4), ACT.Copy))
            for c in range(KT):
                hot_in.take()
                hi_out.up(nc.scalar.activation(yT_hi[:, c, :], uT[:, c, :], ACT.Copy))
            act.wait_ge(sv_normed, NT)
            load_gain(0, a["g_post_mix"])
            load_gain(1, a["g_pre_ffn"])
            for c in range(KT):
                evacuate(T0["a_ret"] + c, mT[:, c, :], ACT.Sigmoid)
            for c in range(KT):
                evacuate(T0["a_sgu"] + c, sgu_gate[:, c, :], ACT.Sigmoid)
            for c in range(KT):
                hot_in.take()
                hi_out.up(nc.scalar.activation(mT_hi[:, c, :], mT[:, c, :], ACT.Copy))
            boundary("norm", T0["out1"], T0["h2"])
            await_evacuated(act, T0["h2"] + 7)
            load_gain(0, a["g_post_ffn"])
            load_gain(1, a["attn_norm"])

            def up_unit(j, i=0):
                t = T0["up1"] + 2 * j
                if j >= 2 or not isinstance(i, int):
                    act.wait_ge(f_made, i * 4 + (j - 1))
                for c in range(2):
                    await_psum(act, t + c, i)
                    col = i * 4 + (j + c * FB)
                    nc.scalar.activation(taps[:, j % 2, c, :], bank(t + c), ACT.Identity,
                                         bias=conv[:, 3, bass.ds(col, 1)],
                                         scale=conv[:, 1, bass.ds(col, 1)]).then_inc(centre, 1)
                give_hi(U0["up1"] + j + 2, i, 4)
                await_evacuated(act, t, i)
                nc.scalar.activation(taps[:, j % 2, 0, :], taps[:, j % 2, 0, :],
                                     ACT.Gelu_apprx_tanh).then_inc(gelu_made, 1)
                act.wait_ge(gated, i * 4 + (j + 1))
                nc.scalar.activation(f_hi[:, bass.ds(i * 4 + j, 1), :], taps[:, j % 2, 0:1, :],
                                     ACT.Copy).then_inc(f_hi_made, 1)

            for j in range(4):
                up_unit(j)
            with act.Fori(1, FB // 4) as i:
                for j in range(4):
                    up_unit(j, i)
            for j in range(FB // 4 * 4, FB):
                up_unit(j)
            for u in range(U0["down1"] + 2, U0["kv_iq"]):
                give_hi(u, started=True)
            boundary("norm", T0["down1"], T0["h3"])

            for n, name in enumerate(("ik_norm_w", "ik_norm_b")):
                act.dma_start(ik_gain[:, n, :], a[name].partition_broadcast(P)).then_inc(ik_gain_loaded, 16)

            def evacuate_pairs(t, dst):
                evacuate(t, dst.rearrange("p (r g d) -> p g r d", r=4, g=2), ACT.Copy,
                         bank(t).rearrange("p (g r d) -> p g r d", g=2, r=4))

            def evacuate_T(base, dst):
                for tt in range(NT):
                    evacuate(base + tt, dst[:, :, tt * P:(tt + 1) * P], ACT.Copy,
                             bank(base + tt).rearrange("p (r n) -> p r n", r=4))

            def index_positive(tt):
                n = (tt + 1) * P
                for h in range(HEADS):
                    s = (tt - 1) * HEADS + h
                    t = T0[f"index{tt}"] + h
                    await_psum(act, t)
                    if s >= HEADS:
                        act.wait_ge(hot, 2 * KT + s - HEADS + 1)
                    nc.scalar.activation(relu[:, h, 0:n], ps[:, t % 8, 0:n],
                                         ACT.Relu).then_inc(evacuated[t % 8], 1)

            for tt in range(NT):
                evacuate(T0["kv_iq"] + tt, kn[:, tt, :], ACT.Copy)
            give_hi(U0["b_q"], started=True)
            for tt in range(NT):
                t = T0["iq_ik"] + tt
                evacuate(t, ib[:, tt, :], ACT.Copy, ps[:, t % 8, 0:IB_W])
            act.wait_ge(ik_stats, NT)
            nc.scalar.activation(ik_stat[:, 40:44], ik_stat[:, 25:33:2], ACT.Sqrt, bias=eps).then_inc(ik_rms, 1)
            for tt in range(NT):
                evacuate_pairs(T0["b_q"] + tt, qn[:, tt, :])
            for tt in range(NT):
                t = T0["b_kv"] + tt
                evacuate(t, bkv[:, tt, :], ACT.Copy, ps[:, t % 8, 0:2 * P])
            evacuate_T(T0["i_T"], qT_a)
            evacuate(T0["i_T"] + 4, ikT[:, :], ACT.Copy)
            index_positive(1)
            evacuate_T(T0["b_T"], qT_b)
            evacuate(T0["b_T"] + 4, bkT[:, :], ACT.Copy)
            for c in range(2):
                evacuate(G_B[c], sig_b[:, c, :], ACT.Sigmoid)
            index_positive(2)
            for tt in range(NT):
                evacuate_pairs(T0["a_q"] + tt, qn[:, tt, :])
            index_positive(3)
            for c in range(2, KT):
                evacuate(G_B[c], sig_b[:, c, :], ACT.Sigmoid)
            evacuate_T(T0["a_T"], qT_a)
            evacuate(T0["a_T"] + 4, akT[:, :], ACT.Copy)
            act.wait_ge(hot, 2 * KT + (NT - 1) * HEADS)

            def attention(events, base, first_key, branch):
                for n, (kind, s) in enumerate(events):
                    t = base + n
                    if kind == "logits":
                        tt, h = s // HEADS, s % HEADS
                        nk = tt + 1 - first_key(tt)
                        if h == 0 and (tt >= 2 or branch):
                            act.wait_ge(o2_made, NT * branch + tt - 1)
                        await_evacuated(act, t)
                        nc.scalar.activation(probs[:, s % 4, 0:nk * P], probs[:, s % 4, 0:nk * P], ACT.Exp,
                                             bias=nm[:, tt % 2, h:h + 1], scale=-1.0,
                                             accum_out=rs[:, tt % 2, h:h + 1]).then_inc(probs_made, 1)
                        if branch and NT <= s < 2 * NT:
                            k = s - NT
                            hi_out.up(nc.scalar.activation(oTb_hi[:, k, :], oTb[:, k, :], ACT.Copy))
                    elif kind == "values":
                        tt, h = s // HEADS, s % HEADS
                        if h == HEADS - 1 and branch == 0:
                            act.wait_ge(sinks_arg, tt + 1)
                            nc.scalar.activation(sink_e[:, tt % 2, :], sink_e[:, tt % 2, :],
                                                 ACT.Exp).then_inc(sinks_exp, 1)
                        if h == 0 and tt >= 2:
                            await_psum(act, base + events.index(("out_T", tt - 2)))
                        await_psum(act, t)
                        nc.scalar.activation(o2[:, tt % 2, h * HD:(h + 1) * HD], ps[:, t % 8, 0:HD],
                                             ACT.Copy).then_inc(evacuated[t % 8], 1)
                    elif kind == "out_T" and branch == 0:
                        evacuate(t, oTb[:, :, s * P:(s + 1) * P], ACT.Copy,
                                 bank(t).rearrange("p (k n) -> p k n", k=4))
                    elif kind == "out_T":
                        await_psum(act, t)
                        hi_out.up(nc.scalar.activation(oTa_hi[:, :, s * P:(s + 1) * P],
                                                       bank(t).rearrange("p (k n) -> p k n", k=4), ACT.Copy))
                    elif kind == "column" and branch == 0:
                        evacuate(t, sig_a[:, s, :], ACT.Copy)

            attention(SWA, T0["swa"], lambda tt: max(tt - 1, 0), 0)
            await_evacuated(act, T0["swa"] + SWA.index(("out_T", NT - 1)))
            attention(DSA, T0["dsa"], lambda tt: 0, 1)
            await_evacuated(act, G_A[KT - 1])
            nc.scalar.activation(sig_a[:, :, :], sig_a[:, :, :], ACT.Sigmoid).then_inc(sigmoids_made, 1)
            await_evacuated(act, T0["dsa"] + DSA.index(("logits", NT * HEADS - 1)))
            load_gain(0, a["mlp_norm"])
            load_gain(1, a["final_norm"])
            hot_in.n += (NT - 1) * HEADS
            for c in range(KT):
                hot_in.take()
                hi_out.up(nc.scalar.activation(m2_hi[:, c, :], sig_a[:, c, :], ACT.Copy))
            boundary("plain", T0["out2"], T0["h4"])
            for half in range(2):
                with act.Fori(0, 2) as i:
                    for j in range(8):
                        t = T0[f"up2_{half}"] + j
                        await_evacuated(act, t, i)
                        nc.scalar.activation(f2_t[:, j % 4, :], f2_t[:, j % 4, :], ACT.Square).then_inc(squared, 1)
                        act.wait_ge(squared, i * 8 + (16 * half + j + 1))
                        nc.scalar.activation(f2_hi[:, bass.ds(i * 8 + j, 1), :], f2_t[:, j % 4:j % 4 + 1, :],
                                             ACT.Copy).then_inc(f2_hi_made, 1)
                        if j % 2:
                            give_hi(U0[f"up2_{half}"] + j // 2 + 2, i, 4)
                after = U0["up2_1"] if half == 0 else N_UNITS
                for u in range(U0[f"down2_{half}"] + 2, min(after + 2, N_UNITS)):
                    give_hi(u, started=True)
            boundary("plain", T0["down2_1"], None)

        @block.vector
        def _(dve):
            step = Count(dve, dve_step)
            rms_in = Count(dve, rms_made)
            h_out = Count(dve, h_made)
            hi_in = Count(dve, hi_made)
            hot_out = Count(dve, hot)
            lo_out = Count(dve, lo_made)
            V = nc.vector

            def boundary(kind, tin, tout, post, pre):
                for which, tt in STEPS:
                    c = 2 * tt + (which == "B")
                    tok = slice(tt * P, (tt + 1) * P)
                    if which == "A" and kind == "norm":
                        rms_in.take()
                        step.up(V.reciprocal(rstd[:, c:c + 1], rms[:, c:c + 1]))
                        step.wait()
                        for half in range(2):
                            t = tin + 2 * tt + half
                            V.scalar_tensor_tensor(h_added[:, 4 * half:4 * half + 4, tok],
                                                   bank(t).rearrange("p (k n) -> p k n", k=4), rstd[:, c:c + 1],
                                                   gain[:, post, half * 512:half * 512 + 512].rearrange(
                                                       "p (k n) -> p k n", k=4),
                                                   ALU.mult, ALU.mult).then_inc(evacuated[t % 8], 1)
                        if tt not in POOL_ADDS:
                            for half in range(2):
                                await_evacuated(dve, tin + 2 * tt + half)
                            row = x[:, tt, :].rearrange("p (k n) -> p k n", k=KT)
                            V.tensor_tensor(row, row, h_added[:, :, tok], ALU.add).then_inc(x_added, 1)
                    elif which == "A" and kind == "plain":
                        for half in range(2):
                            t = tin + 2 * tt + half
                            cc = slice(half * 512, half * 512 + 512)
                            await_psum(dve, t)
                            V.tensor_tensor(x[:, tt, cc], bank(t), x[:, tt, cc], ALU.add).then_inc(evacuated[t % 8], 1)
                    elif which == "B":
                        rms_in.take()
                        if kind == "none":
                            dve.wait_ge(x_loaded[tt], 16)
                        elif kind == "plain":
                            for half in range(2):
                                await_evacuated(dve, tin + 2 * tt + half)
                        step.up(V.reciprocal(rstd[:, c:c + 1], rms[:, c:c + 1]))
                        step.wait()
                        if tout is None:
                            V.scalar_tensor_tensor(out_rows[:, tt, :], x[:, tt, :], rstd[:, c:c + 1], gain[:, pre, :],
                                                   ALU.mult, ALU.mult).then_inc(out_made, 1)
                        else:
                            row, g = [r.rearrange("p (k n) -> p k n", k=KT) for r in (x[:, tt, :], gain[:, pre, :])]
                            h_out.up(V.scalar_tensor_tensor(h_rows[:, :, tok], row, rstd[:, c:c + 1], g,
                                                            ALU.mult, ALU.mult))
                        if kind == "none" and tt == 1:
                            dve.wait_ge(hi_given, 1)
                            V.tensor_tensor(w_lo[:, 0, 0:UNIT // 2], raw[:, 0, 0:UNIT // 2],
                                            w_hi[:, 0, 0:UNIT // 2].bitcast(f32), ALU.subtract).then_inc(first_low, 1)
                    elif which == "C" and tout is not None:
                        for half in range(2):
                            t = tout + 2 * tt + half
                            dst = (slice(None), slice(4 * half, 4 * half + 4), slice(tt * P, (tt + 1) * P))
                            hi_in.take()
                            V.tensor_tensor(hT_lo[dst], bank(t).rearrange("p (k n) -> p k n", k=4),
                                            hT_hi[dst].bitcast(f32), ALU.subtract).then_inc(evacuated[t % 8], 1)

            V.memset(eps, EPS).then_inc(eps_set, 1)
            dve.wait_ge(gains_loaded, 16)
            boundary("none", None, T0["h1"], None, 0)

            dve.wait_ge(tables_loaded, 16 * 9)
            step.up(V.tensor_scalar(gm[0], lg, -1.0, None, ALU.mult))
            step.up(V.tensor_scalar(nsink, sink, -1.0, None, ALU.mult))
            step.wait()
            V.tensor_tensor(gm[1], gm[0], lg, ALU.min).then_inc(gamma_arg, 1)
            dve.wait_ge(gamma_exp, 1)
            step.up(V.tensor_scalar(gm[3], gm[2], 2.0, None, ALU.add))
            step.wait()
            step.up(V.reciprocal(gm[4], gm[3]))
            step.wait()
            step.up(V.tensor_tensor(gm[3], gm[2], gm[4], ALU.mult))
            step.wait()
            step.up(V.tensor_tensor(gm[4], gm[3], gm[3], ALU.mult))
            step.wait()
            step.up(V.tensor_scalar(gm[5], gm[4], 1.0 / 17, None, ALU.mult))
            for odd in range(15, 1, -2):
                step.wait()
                step.up(V.scalar_tensor_tensor(gm[5], gm[5], 1.0 / odd, gm[4], ALU.add, ALU.mult))
            step.wait()
            step.up(V.scalar_tensor_tensor(gm[6], gm[5], 1.0, gm[3], ALU.add, ALU.mult))
            step.up(V.tensor_scalar(gm[7], lg, 0.0, None, ALU.min))
            step.wait()
            step.up(V.scalar_tensor_tensor(lg, gm[6], -2.0, gm[7], ALU.mult, ALU.add))
            step.wait()
            step.up(V.tensor_scalar(gm[0], lg, -1.0, None, ALU.mult))

            rotated = {name: Count(dve, s) for name, s in (("qk", qk_rotated), ("i", i_rotated),
                                                           ("b", b_rotated), ("a", a_rotated))}
            last_rope = [step]

            def rope(src, dst, heads, half, table, tt, tmp, tile_of, count):
                n = heads * 2 * half
                view = [P, heads, 2, half]
                c = table[:, tt, 0, None, None, :].broadcast_to(view)
                s = table[:, tt, None, 1:3, :].broadcast_to(view)
                ta, tb = [tmp[:, k, 0:n].rearrange("p (h a d) -> p h a d", h=heads, a=2) for k in range(2)]
                t4 = src.rearrange("p (h a d) -> p h a d", h=heads, a=2)
                last_rope[0].wait()
                last_rope[0] = count
                step.up(V.tensor_tensor(ta, t4, c, ALU.mult))
                last = V.tensor_tensor(tb, t4[:, :, ::-1, :], s, ALU.mult)
                if tile_of is None:
                    step.up(last)
                else:
                    last.then_inc(evacuated[tile_of % 8], 1)
                    await_evacuated(dve, tile_of)
                step.wait()
                count.up(V.tensor_tensor(dst, tmp[:, 0, 0:n], tmp[:, 1, 0:n], ALU.add))

            for w in range(2):
                for tt in range(NT):
                    t = T0["qkvg"] + 4 * w + tt
                    await_psum(dve, t)
                    rope(bank(t), qk[:, w, tt, :], RET_H, RET_DK // 2, rope1, tt, rope_t, t, rotated["qk"])

            def decay_args(h):
                if h:
                    dve.wait_ge(decay_arg, h)
                step.up(V.tensor_scalar(decay[:, h % 2, :], distance[:, :], 0.0, lg[:, h:h + 1], ALU.max, ALU.mult))
                step.up(V.tensor_scalar(decay[:, 2, :], distance[:, :], 0.0, gm[0][:, 4 + h:5 + h], ALU.min, ALU.mult))
                step.wait()
                V.tensor_tensor(decay[:, h % 2, :], decay[:, h % 2, :], decay[:, 2, :], ALU.add).then_inc(decay_arg, 1)

            decay_args(0)
            decay_args(1)
            t = T0["ret"]
            for kind, h in RETENTION:
                if kind == "scores":
                    dve.wait_ge(decay_made, h + 1)
                    for mb in range(NT):
                        if h >= 2 and mb == 0:
                            await_psum(dve, t - 1)
                        await_psum(dve, t)
                        V.scalar_tensor_tensor(sT[:, h % 2, mb, :], bank(t), RET_DK ** -0.5,
                                               decay[:, h % 2, (NT - 1 - mb) * P:(NT - 1 - mb) * P + S],
                                               ALU.mult, ALU.mult).then_inc(evacuated[t % 8], 1)
                        t += 1
                    if h + 2 < RET_H:
                        for b in range(t - NT, t):
                            await_evacuated(dve, b)
                        decay_args(h + 2)
                else:
                    for pair in range(2):
                        await_evacuated(dve, t)
                        for nn in range(2):
                            at_ = h * NT + 2 * pair + nn
                            if at_ == 0:
                                await_evacuated(dve, T0["ret"] + 2 * NT - 1)
                            else:
                                dve.wait_ge(o_stats, at_)
                            six = o_stat[:, 6 * (at_ % 2):6 * (at_ % 2) + 6]
                            step.up(V.bn_stats(six, o[:, 2 * pair + nn, h, :]))
                            step.wait()
                            V.bn_aggr(o_stat[:, 12 + 2 * at_:14 + 2 * at_], six).then_inc(o_stats, 1)
                        t += 1
            dve.wait_ge(o_rms, 1)
            step.up(V.reciprocal(o_stat[:, 44:60], o_stat[:, 60:76]))
            step.wait()
            for tt in range(NT):
                for h in range(RET_H):
                    n = h * NT + tt
                    step.up(V.tensor_scalar(o[:, tt, h, :], o[:, tt, h, :], o_stat[:, 12 + 2 * n:13 + 2 * n],
                                            o_stat[:, 44 + n:45 + n], ALU.subtract, ALU.mult))
                step.wait()
                row = o[:, tt, :, :].rearrange("p h e -> p (h e)")
                V.tensor_tensor(row, row, silu_g[:, tt, :], ALU.mult).then_inc(o_gated, 1)

            for tt in range(NT):
                for b in range(2):
                    await_evacuated(dve, T0["sv"] + 4 * b + tt)
                    six = 12 * tt + 6 * b
                    step.up(V.bn_stats(sv_stat[:, six:six + 6], sv[:, tt, b * 512:b * 512 + 512]))
                step.wait()
                V.bn_aggr(sv_stat[:, 48 + 2 * tt:50 + 2 * tt],
                          sv_stat[:, 12 * tt:12 * tt + 12]).then_inc(sv_stats, 1)
            dve.wait_ge(sv_rms, 1)
            step.up(V.reciprocal(sv_stat[:, 68:72], sv_stat[:, 64:68]))
            step.wait()
            dve.wait_ge(gains_loaded, 16 * 3)
            for tt in range(NT):
                step.up(V.tensor_scalar(sv[:, tt, :], sv[:, tt, :], sv_stat[:, 48 + 2 * tt:49 + 2 * tt],
                                        sv_stat[:, 68 + tt:69 + tt], ALU.subtract, ALU.mult))
                step.wait()
                step.up(V.tensor_tensor(sv[:, tt, :], sv[:, tt, :], gain[:, 0, :], ALU.mult))
                step.wait()
                V.tensor_tensor(sv[:, tt, :], sv[:, tt, :], gain[:, 1, :], ALU.add).then_inc(sv_normed, 1)
            for tt in range(NT):
                for half in range(2):
                    t = T0["o_T"] + 2 * tt + half
                    dst = (slice(None), slice(4 * half, 4 * half + 4), slice(tt * P, (tt + 1) * P))
                    hi_in.take()
                    V.tensor_tensor(oT_lo[dst], bank(t).rearrange("p (k n) -> p k n", k=4),
                                    oT_hi[dst].bitcast(f32), ALU.subtract).then_inc(evacuated[t % 8], 1)

            def y_low(c):
                hi_in.take()
                lo_out.up(V.tensor_tensor(yT_lo[:, c, :], uT[:, c, :], yT_hi[:, c, :].bitcast(f32), ALU.subtract))

            dve.wait_ge(spatial_b_loaded, 16)
            for c in range(KT):
                t = T0["mix"] + c
                await_psum(dve, t)
                V.tensor_tensor(mix_t[:, c % 2, :].rearrange("p (n q) -> p n q", n=NT),
                                bank(t).rearrange("p (n q) -> p n q", n=NT),
                                spatial_b[:, None, c // 2, :].broadcast_to([P, NT, P]),
                                ALU.add).then_inc(evacuated[t % 8], 1)
                await_evacuated(dve, t)
                await_evacuated(dve, T0["u"] + c)
                hot_out.up(V.tensor_tensor(uT[:, c, :], mix_t[:, c % 2, :], uT[:, c, :], ALU.mult))
                if c:
                    y_low(c - 1)
            y_low(KT - 1)

            def gate(t, gates, g_ticket, c):
                await_psum(dve, t)
                await_evacuated(dve, g_ticket)
                V.tensor_tensor(gates[:, c, :], bank(t), gates[:, c, :], ALU.mult).then_inc(evacuated[t % 8], 1)

            def gate_and_merge(base, gates, other, merged, g_tickets, hi, lo, other_tickets):
                def low(c):
                    hi_in.take()
                    lo_out.up(V.tensor_tensor(lo[:, c, :], merged[:, c, :], hi[:, c, :].bitcast(f32), ALU.subtract))

                for c in range(KT):
                    gate(base + c, gates, g_tickets[c], c)
                    await_evacuated(dve, base + c)
                    await_evacuated(dve, other_tickets[c])
                    hot_out.up(V.tensor_tensor(merged[:, c, :], gates[:, c, :], other[:, c, :], ALU.add))
                    if c:
                        low(c - 1)
                low(KT - 1)

            def columns(phase):
                return [T0[phase] + c for c in range(KT)]

            for c in range(KT):
                gate(T0["y_ret"] + c, mT, T0["a_ret"] + c, c)
            gate_and_merge(T0["y_sgu"], sgu_gate, mT, mT, columns("a_sgu"), mT_hi, mT_lo, columns("y_ret"))
            dve.wait_ge(gains_loaded, 16 * 5)
            boundary("norm", T0["out1"], T0["h2"], 0, 1)

            def up_unit(j, i=0):
                t = T0["up1"] + 2 * j
                for c in range(2):
                    tap = taps[:, j % 2, c, :]
                    col = i * 4 + (j + c * FB)
                    dve.wait_ge(centre, i * 8 + (2 * j + c + 1))
                    V.scalar_tensor_tensor(tap[:, 1:S], ps[:, (t + c) % 8, 0:S - 1], conv[:, 0, bass.ds(col, 1)],
                                           tap[:, 1:S], ALU.mult, ALU.add).then_inc(left, 1)
                    dve.wait_ge(left, i * 8 + (2 * j + c + 1))
                    V.scalar_tensor_tensor(tap[:, 0:S - 1], ps[:, (t + c) % 8, 1:S], conv[:, 2, bass.ds(col, 1)],
                                           tap[:, 0:S - 1], ALU.mult, ALU.add).then_inc(evacuated[(t + c) % 8], 1)
                dve.wait_ge(gelu_made, i * 4 + (j + 1))
                await_evacuated(dve, t + 1, i)
                V.tensor_tensor(taps[:, j % 2, 0, :], taps[:, j % 2, 0, :], taps[:, j % 2, 1, :],
                                ALU.mult).then_inc(gated, 1)
                dve.wait_ge(f_hi_made, i * 4 + (j + 1))
                at_ = bass.ds(i * 4 + j, 1)
                V.tensor_tensor(f_lo[:, at_, :], taps[:, j % 2, 0:1, :], f_hi[:, at_, :].bitcast(f32),
                                ALU.subtract).then_inc(f_made, 1)

            with dve.Fori(0, FB // 4) as i:
                for j in range(4):
                    up_unit(j, i)
            for j in range(FB // 4 * 4, FB):
                up_unit(j)
            dve.wait_ge(gains_loaded, 16 * 7)
            boundary("norm", T0["down1"], T0["h3"], 0, 1)

            for tt in range(NT):
                await_evacuated(dve, T0["iq_ik"] + tt)
                step.up(V.bn_stats(ik_stat[:, 6 * tt:6 * tt + 6], ib[:, tt, 256:256 + HD]))
                step.wait()
                V.bn_aggr(ik_stat[:, 24 + 2 * tt:26 + 2 * tt], ik_stat[:, 6 * tt:6 * tt + 6]).then_inc(ik_stats, 1)
            dve.wait_ge(ik_rms, 1)
            step.up(V.reciprocal(ik_stat[:, 44:48], ik_stat[:, 40:44]))
            step.wait()
            for tt in range(NT):
                key = ib[:, tt, 256:256 + HD]
                step.up(V.tensor_scalar(key, key, ik_stat[:, 24 + 2 * tt:25 + 2 * tt], ik_stat[:, 44 + tt:45 + tt],
                                        ALU.subtract, ALU.mult))
                step.wait()
                if tt == 0:
                    dve.wait_ge(ik_gain_loaded, 32)
                step.up(V.tensor_tensor(key, key, ik_gain[:, 0, :], ALU.mult))
                step.wait()
                step.up(V.tensor_tensor(key, key, ik_gain[:, 1, :], ALU.add))
                step.wait()
                rope(key, ik2[:, tt, 0, :], 1, HD // 2, rope2, tt, rope_u, None, step)
                step.wait()
                rope(kn[:, tt, 256:512], kn[:, tt, 256:512], 4, HD // 2, rope2, tt, rope_u, None, rotated["i"])
                rope(ib[:, tt, 0:256], ib[:, tt, 0:256], 4, HD // 2, rope2, tt, rope_u, None, rotated["i"])
                rotated["i"].up(V.tensor_copy(ik2[:, tt, 1, :], ik2[:, tt, 0, :]))
                w8 = ib[:, tt, 256 + HD:256 + HD + HEADS]
                step.up(V.tensor_scalar(w8, w8, HEADS ** -0.5 * HD ** -0.5, None, ALU.mult))
            for tt in range(NT):
                await_evacuated(dve, T0["b_q"] + tt)
                rope(qn[:, tt, :], qn[:, tt, :], HEADS, HD // 2, rope2, tt, rope_u, None, rotated["b"])
                await_evacuated(dve, T0["b_kv"] + tt)
                rope(bkv[:, tt, 0:P], bkv[:, tt, 0:P], KV_HEADS, HD // 2, rope2, tt, rope_u, None, rotated["b"])
            rotated["b"].wait()

            step.up(V.tensor_copy(mask[:, 0, 0:P], band[:, P:2 * P]))
            for tt in range(1, NT):
                if tt == NT - 1:
                    step.wait()
                    for n in range(NT):
                        await_evacuated(dve, T0["a_q"] + n)
                        rope(qn[:, n, :], qn[:, n, :], HEADS, HD // 2, rope2, n, rope_u, None, rotated["a"])
                        rope(kn[:, n, 0:P], kn[:, n, 0:P], KV_HEADS, HD // 2, rope2, n, rope_u, None, rotated["a"])
                    rotated["a"].wait()
                n = (tt + 1) * P
                for h in range(HEADS):
                    s = (tt - 1) * HEADS + h
                    await_evacuated(dve, T0[f"index{tt}"] + h)
                    w = ib[:, tt, 256 + HD + h:257 + HD + h]
                    if h == 0:
                        hot_out.up(V.tensor_scalar(score[:, 0:n], relu[:, h, 0:n], w, None, ALU.mult))
                    else:
                        hot_out.wait()
                        hot_out.up(V.scalar_tensor_tensor(score[:, 0:n], relu[:, h, 0:n], w, score[:, 0:n],
                                                          ALU.mult, ALU.add))
                hot_out.wait()
                step.up(V.tensor_tensor(score[:, tt * P:n], score[:, tt * P:n], band[:, P:2 * P], ALU.add))
                for r in range(TOPK // 8):
                    src = score if r == 0 else work
                    step.wait()
                    step.up(V.max(top[:, 0:8], src[:, 0:n]))
                    step.wait()
                    if r < TOPK // 8 - 1:
                        step.up(V.match_replace(work[:, 0:n], top[:, 0:8], src[:, 0:n], LOWEST))
                kth = top[:, 7:8]
                step.up(V.tensor_scalar(above[:, 0:n], score[:, 0:n], kth, 0.0, ALU.is_gt, ALU.add,
                                        accum_out=top[:, 8:9]))
                step.up(V.tensor_scalar(equal[:, 0:n], score[:, 0:n], kth, None, ALU.is_equal))
                step.wait()
                step.up(V.tensor_scalar(top[:, 9:10], top[:, 8:9], -1.0, float(TOPK), ALU.mult, ALU.add))
                step.up(V.tensor_tensor_scan(upto[:, 0:n], equal[:, 0:n], equal[:, 0:n], 0.0, ALU.add, ALU.max))
                step.wait()
                step.up(V.scalar_tensor_tensor(equal[:, 0:n], upto[:, 0:n], top[:, 9:10], equal[:, 0:n],
                                               ALU.is_le, ALU.mult))
                step.wait()
                step.up(V.tensor_tensor(above[:, 0:n], above[:, 0:n], equal[:, 0:n], ALU.add))
                step.wait()
                step.up(V.tensor_scalar(mask[:, tt, 0:n], above[:, 0:n], -1.0, -NEG, ALU.add, ALU.mult))
            def attention(events, base, first_key, mask_of, branch):
                for n, (kind, s) in enumerate(events):
                    t = base + n
                    if kind == "logits":
                        tt, h = s // HEADS, s % HEADS
                        nk = tt + 1 - first_key(tt)
                        if s >= 4:
                            await_psum(dve, base + events.index(("probs_T", s - 4)))
                        await_psum(dve, t)
                        V.tensor_tensor_reduce(out=probs[:, s % 4, 0:nk * P], in0=ps[:, t % 8, 0:nk * P],
                                               in1=mask_of(tt), scale=-(HD ** -0.5),
                                               scalar=nsink[:, h:h + 1] if branch == 0 else -LOWEST,
                                               op0=ALU.add, op1=ALU.min,
                                               accum_out=nm[:, tt % 2, h:h + 1]).then_inc(evacuated[t % 8], 1)
                        if branch and NT < s <= 2 * NT:
                            k = s - NT - 1
                            hi_in.take()
                            lo_out.up(V.tensor_tensor(oTb_lo[:, k, :], oTb[:, k, :], oTb_hi[:, k, :].bitcast(f32),
                                                      ALU.subtract))
                    elif kind == "probs_T":
                        tt = s // HEADS
                        nk = tt + 1 - first_key(tt)
                        if s >= 2:
                            await_psum(dve, base + events.index(("values", s - 2)))
                        await_psum(dve, t)
                        V.tensor_copy(probs_T[:, s % 2, 0:nk * P], ps[:, t % 8, 0:nk * P]).then_inc(evacuated[t % 8], 1)
                    elif kind == "values":
                        tt, h = s // HEADS, s % HEADS
                        if h < HEADS - 1:
                            continue
                        b = tt % 2
                        if branch == 0:
                            await_evacuated(dve, base + events.index(("logits", s)))
                            V.tensor_tensor(sink_e[:, b, :], nm[:, b, :], sink, ALU.add).then_inc(sinks_arg, 1)
                            dve.wait_ge(sinks_exp, tt + 1)
                            step.up(V.tensor_tensor(rs[:, b, :], rs[:, b, :], sink_e[:, b, :], ALU.add))
                            step.wait()
                        dve.wait_ge(probs_made, 32 * branch + s + 1)
                        step.up(V.reciprocal(ri[:, b, :], rs[:, b, :]))
                        for back in range(HEADS):
                            await_evacuated(dve, base + events.index(("values", s - back)))
                        step.wait()
                        v3 = o2[:, b, :].rearrange("p (h d) -> p h d", h=HEADS)
                        V.tensor_tensor(v3, v3, ri[:, b, :, None].broadcast_to([P, HEADS, HD]),
                                        ALU.mult).then_inc(o2_made, 1)
                    elif kind == "out_T" and branch:
                        hi_in.take()
                        dst = (slice(None), slice(None), slice(s * P, (s + 1) * P))
                        V.tensor_tensor(oTa_lo[dst], bank(t).rearrange("p (k n) -> p k n", k=4),
                                        oTa_hi[dst].bitcast(f32), ALU.subtract).then_inc(evacuated[t % 8], 1)
                    elif kind == "column" and branch:
                        gate(Y_B[s], sig_b, G_B[s], s)

            attention(SWA, T0["swa"], lambda tt: max(tt - 1, 0),
                      lambda tt: band[:, 0:2 * P] if tt else band[:, P:2 * P], 0)
            attention(DSA, T0["dsa"], lambda tt: 0, lambda tt: mask[:, tt, 0:(tt + 1) * P], 1)
            dve.wait_ge(sigmoids_made, 1)
            gate_and_merge(T0["y_a"], sig_a, sig_b, sig_a, G_A, m2_hi, m2_lo, Y_B)
            dve.wait_ge(gains_loaded, 16 * 9)
            boundary("plain", T0["out2"], T0["h4"], None, 0)
            for half in range(2):
                with dve.Fori(0, 2) as i:
                    for j in range(8):
                        t = T0[f"up2_{half}"] + j
                        await_psum(dve, t, i)
                        if j:
                            dve.wait_ge(f2_made, i * 8 + (16 * half + j))
                        V.tensor_scalar(f2_t[:, j % 4, :], bank(t), 0.0, None, ALU.max).then_inc(evacuated[t % 8], 1)
                        dve.wait_ge(f2_hi_made, i * 8 + (16 * half + j + 1))
                        at_ = bass.ds(i * 8 + j, 1)
                        V.tensor_tensor(f2_lo[:, at_, :], f2_t[:, j % 4:j % 4 + 1, :], f2_hi[:, at_, :].bitcast(f32),
                                        ALU.subtract).then_inc(f2_made, 1)
                if half == 0:
                    for k in range(8):
                        t = T0["down2_0"] + k
                        cc = slice(k % 2 * 512, k % 2 * 512 + 512)
                        await_psum(dve, t)
                        V.tensor_tensor(x[:, k // 2, cc], bank(t), x[:, k // 2, cc],
                                        ALU.add).then_inc(evacuated[t % 8], 1)
            boundary("plain", T0["down2_1"], None, None, 1)


_INS = {"x": "x", "g_pre_mix": "g_pre_mix", "w_in": "w_in", "ret_decay_logit": "ret_decay_logit",
        "sgu_ln_g": "sgu_ln_g", "sgu_ln_b": "sgu_ln_b", "w_spatial": "w_spatial", "b_spatial": "b_spatial",
        "w_ret_o": "w_ret_o", "w_sgu_o": "w_sgu_o", "w_out": "w_out", "g_post_mix": "g_post_mix",
        "g_pre_ffn": "g_pre_ffn", "w_up": "w_up", "conv_w": "conv_w", "conv_b": "conv_b",
        "w_down": "w_down", "g_post_ffn": "g_post_ffn", "attn_norm": "attn_norm_w_2",
        "w_in2": "w_in_2", "ik_norm_w": "idx_k_norm_w_2", "ik_norm_b": "idx_k_norm_b_2",
        "sinks": "sinks_2", "w_branch_a": "w_branch_a_2", "w_branch_b": "w_branch_b_2",
        "w_out2": "w_out_2", "mlp_norm": "mlp_norm_w_2", "w_up2": "w_up_2", "w_down2": "w_down_2",
        "final_norm": "final_norm_w_2"}
_LAYERED = {"attn_norm", "w_in2", "ik_norm_w", "ik_norm_b", "w_branch_a", "w_branch_b", "w_out2",
            "mlp_norm", "w_up2", "w_down2"}


def _tables(np):
    def rope(half):
        inv = (1.0 / (10000.0 ** (np.arange(half, dtype=np.float64) / half))).astype(np.float32)
        ang = np.arange(S, dtype=np.float32)[:, None] * inv[None, :]
        c, s = np.cos(ang.astype(np.float64)), np.sin(ang.astype(np.float64))
        t = np.stack([c, -s, s], axis=1).astype(np.float32)
        return np.ascontiguousarray(t.reshape(NT, P, 3, half).transpose(1, 0, 2, 3))

    q, k = np.arange(P)[:, None], np.arange(P)[None, :]
    band = np.concatenate([np.where(k > q, 0.0, NEG), np.where(k <= q, 0.0, NEG)], axis=1)
    distance = np.arange(STRIP)[None, :] - (NT - 1) * P - np.arange(P)[:, None]
    return {"rope1": rope(RET_DK // 2), "rope2": rope(HD // 2), "band": band.astype(np.float32),
            "distance": distance.astype(np.float32), "ident": np.eye(P, dtype=np.float32)}


def kernel(**inputs):
    import numpy as _np
    import concourse.bacc as _bacc
    from concourse import mybir as _mybir
    from concourse.bass_utils import run_bass_kernel_spmd as _run

    nc = _bacc.Bacc("TRN2", target_bir_lowering=False, num_devices=1)
    arrays, a = {}, {}

    def declare(name, array):
        arrays[f"in_{name}"] = array
        a[name] = nc.dram_tensor(f"in_{name}", array.shape, _mybir.dt.from_np(array.dtype),
                                 kind="ExternalInput").ap()

    for name, given in _INS.items():
        declare(name, _np.ascontiguousarray(inputs[given]))
        if name in _LAYERED:
            a[name] = a[name][0]
    for name, table in _tables(_np).items():
        declare(name, table)
    out = nc.dram_tensor("out", (1, S, D), _mybir.dt.float32, kind="ExternalOutput").ap()
    two_blocks(nc, a, out)
    r = _run(nc, [arrays], core_ids=[0])
    return r.results[0]["out"]
```
